# Optimizing a Trainium2 kernel written in Bass

```python
import jax, jax.numpy as jnp
from jax import lax
import numpy as np

D_MODEL = 1024
BATCH = 1
SEQ = 1024
DEPTH = 1

D_MIX = D_MODEL
ATTN_HEADS = 8
HEAD_DIM = 64
D_ATTN = ATTN_HEADS * HEAD_DIM
D_CONV = D_MIX - D_ATTN
CONV_GROUPS = 8
CONV_K = 31
DILATED_PATTERNS = ((128, 1), (512, 4), (2048, 16))
BLK = 128
D_FF = 2816
D_IN = 3 * D_ATTN + 2 * D_CONV
EPS = 1e-6

kernel_name = "hybrid_dilated_attn_conformer_conv_macaron"

def _rms(x, g):
    xf = x.astype(jnp.float32)
    y = xf * lax.rsqrt(jnp.mean(xf * xf, axis=-1, keepdims=True) + EPS)
    return (y * g.astype(jnp.float32)).astype(x.dtype)

def _layernorm(x, g, b):
    xf = x.astype(jnp.float32)
    mu = jnp.mean(xf, axis=-1, keepdims=True)
    var = jnp.mean(jnp.square(xf - mu), axis=-1, keepdims=True)
    y = (xf - mu) * lax.rsqrt(var + EPS)
    return (y * g.astype(jnp.float32) + b.astype(jnp.float32)).astype(x.dtype)

def _swiglu(x, w_gate, w_up, w_down):
    return (jax.nn.silu(x @ w_gate) * (x @ w_up)) @ w_down

def _banded_causal_attn(q, k, v, steps):
    Bp, L, H, Dh = q.shape
    N = L // BLK
    qb = q.reshape(Bp, N, BLK, H, Dh)
    kb = k.reshape(Bp, N, BLK, H, Dh)
    vb = v.reshape(Bp, N, BLK, H, Dh)

    def with_prev(a):
        prev = jnp.concatenate([jnp.zeros_like(a[:, :1]), a[:, :-1]], axis=1)
        return jnp.concatenate([prev, a], axis=2)

    kk, vv = with_prev(kb), with_prev(vb)
    s = jnp.einsum('bnqhd,bnkhd->bnhqk', qb, kk,
                   preferred_element_type=jnp.float32) * (Dh ** -0.5)
    qi = jnp.arange(BLK)[:, None]
    ci = jnp.arange(2 * BLK)[None, :]
    dist = BLK + qi - ci
    band = (dist >= 0) & (dist <= steps)
    first = (jnp.arange(N) == 0)[:, None, None] & (ci < BLK)[None]
    mask = band[None] & jnp.logical_not(first)
    s = jnp.where(mask[None, :, None], s, jnp.float32(-1e30))
    m = jnp.max(s, axis=-1, keepdims=True)
    p = jnp.exp(s - m)
    l = jnp.sum(p, axis=-1, keepdims=True)
    o = jnp.einsum('bnhqk,bnkhd->bnqhd', (p / l).astype(v.dtype), vv,
                   preferred_element_type=jnp.float32)
    lse = (m + jnp.log(l))[..., 0]
    return o.reshape(Bp, L, H, Dh), lse.transpose(0, 1, 3, 2).reshape(Bp, L, H)

def _dilated_causal_attn(q, k, v, window, dilation):
    B, S, H, Dh = q.shape
    span = dilation * BLK
    S_pad = -(-S // span) * span
    L = S_pad // dilation

    def strided(a):
        a = jnp.pad(a, ((0, 0), (0, S_pad - S), (0, 0), (0, 0)))
        return a.reshape(B, L, dilation, H, Dh).transpose(0, 2, 1, 3, 4).reshape(B * dilation, L, H, Dh)

    o, lse = _banded_causal_attn(strided(q), strided(k), strided(v), window // dilation)
    o = o.reshape(B, dilation, L, H, Dh).transpose(0, 2, 1, 3, 4).reshape(B, S_pad, H, Dh)[:, :S]
    lse = lse.reshape(B, dilation, L, H).transpose(0, 2, 1, 3).reshape(B, S_pad, H)[:, :S]
    return o, lse

def _conformer_conv(a, gate, conv_w, conv_b, ln_g, ln_b):
    glu = a * jax.nn.sigmoid(gate)
    y = lax.conv_general_dilated(
        glu, conv_w[:, None, :], window_strides=(1,), padding=[(CONV_K - 1, 0)],
        dimension_numbers=('NWC', 'WIO', 'NWC'), feature_group_count=D_CONV)
    y = y + conv_b
    return jax.nn.silu(_layernorm(y, ln_g, ln_b))

def setup_inputs(seed: int = 0) -> dict:
    key = jax.random.key(seed)
    ks = jax.random.split(key, 20)
    L = DEPTH

    def nrm(k, shape, scale):
        return jax.random.normal(k, shape, jnp.float32) * scale

    def gain(k, shape):
        return 1.0 + 0.02 * jax.random.normal(k, shape, jnp.float32)

    return {
        "x": jax.random.normal(ks[0], (BATCH, SEQ, D_MODEL), jnp.float32),
        "ffn1_norm": gain(ks[1], (L, D_MODEL)),
        "ffn1_w_gate": nrm(ks[2], (L, D_MODEL, D_FF), D_MODEL ** -0.5),
        "ffn1_w_up": nrm(ks[3], (L, D_MODEL, D_FF), D_MODEL ** -0.5),
        "ffn1_w_down": nrm(ks[4], (L, D_FF, D_MODEL), D_FF ** -0.5),
        "mix_norm": gain(ks[5], (L, D_MODEL)),
        "w_in": nrm(ks[6], (L, D_MODEL, D_IN), D_MODEL ** -0.5),
        "q_norm": gain(ks[7], (L, HEAD_DIM)),
        "k_norm": gain(ks[8], (L, HEAD_DIM)),
        "conv_w": nrm(ks[9], (L, CONV_K, D_CONV), CONV_K ** -0.5),
        "conv_b": nrm(ks[10], (L, D_CONV), 0.02),
        "conv_ln_g": gain(ks[11], (L, D_CONV)),
        "conv_ln_b": nrm(ks[12], (L, D_CONV), 0.02),
        "w_out": nrm(ks[13], (L, D_MIX, D_MODEL), D_MIX ** -0.5),
        "ffn2_norm": gain(ks[14], (L, D_MODEL)),
        "ffn2_w_gate": nrm(ks[15], (L, D_MODEL, D_FF), D_MODEL ** -0.5),
        "ffn2_w_up": nrm(ks[16], (L, D_MODEL, D_FF), D_MODEL ** -0.5),
        "ffn2_w_down": nrm(ks[17], (L, D_FF, D_MODEL), D_FF ** -0.5),
    }

def reference(x, ffn1_norm, ffn1_w_gate, ffn1_w_up, ffn1_w_down, mix_norm, w_in, q_norm, k_norm,
              conv_w, conv_b, conv_ln_g, conv_ln_b, w_out, ffn2_norm, ffn2_w_gate, ffn2_w_up,
              ffn2_w_down):
    B, S, _ = x.shape
    h = x
    for l in range(DEPTH):
        h = h + 0.5 * _swiglu(_rms(h, ffn1_norm[l]), ffn1_w_gate[l], ffn1_w_up[l], ffn1_w_down[l])

        u = _rms(h, mix_norm[l]) @ w_in[l]
        q, k, v, ca, cg = jnp.split(
            u, np.cumsum([D_ATTN, D_ATTN, D_ATTN, D_CONV]).tolist(), axis=-1)

        q = _rms(q.reshape(B, S, ATTN_HEADS, HEAD_DIM), q_norm[l])
        k = _rms(k.reshape(B, S, ATTN_HEADS, HEAD_DIM), k_norm[l])
        v = v.reshape(B, S, ATTN_HEADS, HEAD_DIM)
        outs, lses = [], []
        for window, dilation in DILATED_PATTERNS:
            o, lse = _dilated_causal_attn(q, k, v, window, dilation)
            outs.append(o)
            lses.append(lse)
        wts = jax.nn.softmax(jnp.stack(lses, axis=0), axis=0)
        attn = jnp.sum(wts[..., None] * jnp.stack(outs, axis=0), axis=0)
        attn = attn.reshape(B, S, D_ATTN).astype(h.dtype)

        conv = _conformer_conv(ca, cg, conv_w[l], conv_b[l], conv_ln_g[l], conv_ln_b[l])

        h = h + jnp.concatenate([attn, conv], axis=-1) @ w_out[l]

        h = h + 0.5 * _swiglu(_rms(h, ffn2_norm[l]), ffn2_w_gate[l], ffn2_w_up[l], ffn2_w_down[l])
    return h


_drawn_inputs = setup_inputs


def setup_inputs(seed=0):
    import zlib

    import numpy as np

    out = dict(_drawn_inputs(seed))
    spreads = {}
    factors = {'ffn1_norm': 6.081,
     'mix_norm': 5.854,
     'q_norm': 8.0,
     'k_norm': 8.0,
     'conv_b': 29.312,
     'conv_ln_g': 47.432,
     'conv_ln_b': 56.912,
     'ffn2_norm': 7.826}
    for name, (base, spread) in spreads.items():
        noise = np.random.default_rng([zlib.crc32(name.encode()), seed]).standard_normal(out[name].shape)
        drawn = base * np.exp(spread * noise) if base else spread * noise
        out[name] = __import__('jax').numpy.asarray(drawn.astype(out[name].dtype))
    for name, factor in factors.items():
        out[name] = (out[name] * factor).astype(out[name].dtype)
    return out
```

```python
import concourse.bass as bass
from concourse import mybir
from contextlib import ExitStack

F32 = mybir.dt.float32
F32R = mybir.dt.float32r
ALU = mybir.AluOpType
ACT = mybir.ActivationFunctionType
ds = bass.ds

P = 128
D = 1024
SEQ = 1024
DT = D // P
HALF = 512
FF = 2816
FT = FF // P
CHUNKS = FT // 2
HEADS, DH = 8, 64
PAIRS = HEADS // 2
TAPS = 31
EPS = 1e-6
NEG = -1e30
SLOTS = 6
UNIT = 1024

U_FFN1 = 0
U_PROJ = U_FFN1 + 6 * CHUNKS
U_V = U_PROJ + 4 * PAIRS
U_WO = U_V + 4
U_FFN2 = U_WO + DT
UNITS = U_FFN2 + 6 * CHUNKS + 4

FILL = {"ffn1": 0, "proj": CHUNKS, "v": CHUNKS + 4, "wo": CHUNKS + 5, "ffn2": CHUNKS + 7}
FILL45 = {"ffn1": 0, "ffn2": CHUNKS}
BANKUSE = {"ffn1": 0, "proj": 2 * CHUNKS, "ffn2": 2 * CHUNKS + 2 * PAIRS}
DUSE = {"ffn1": 0, "ffn2": 16 * CHUNKS}

C_G = {"ffn1": 0, "proj": 8, "ffn2": 16}
C_CW = 24
C_CB = C_CW + 4 * TAPS
C_LG = C_CB + 4
C_LB = C_LG + 4
C_QG = C_LB + 4
C_KG = C_QG + 1
C_N = C_KG + 1


def build(nc, xT, stream, smalls, ones_mean, ones_head, ones_conv, ident_in, table_in, outT):
    h_spill = nc.dram_tensor("h_spill", (P, DT * SEQ), F32).ap()
    ctx = ExitStack()
    with ctx:
        def sb(name, shape, dt):
            return ctx.enter_context(nc.sbuf_tensor(name, shape, dt))

        def sem(name):
            return ctx.enter_context(nc.semaphore(name))

        xh = sb("xh", [P, 8, SEQ], F32R)
        xl = sb("xl", [P, 8, SEQ], F32R)
        h = sb("h", [P, 8, SEQ], F32)
        wraw = sb("wraw", [P, 2, UNIT], F32)
        wh = sb("wh", [P, SLOTS, UNIT], F32R)
        wl = sb("wl", [P, SLOTS, UNIT], F32R)
        ah = sb("ah", [P, 2, SEQ], F32R)
        al = sb("al", [P, 2, SEQ], F32R)
        y = sb("y", [P, 4, SEQ], F32)
        glu = sb("glu", [P, TAPS - 1 + SEQ], F32)
        tmp = sb("tmp", [P, 4, HALF], F32)
        rt = sb("rt", [P, 4, HALF], F32)
        consts = sb("consts", [P, C_N], F32)
        eps_col = sb("eps_col", [P, 2], F32)
        negqg = sb("negqg", [P, 1], F32)
        om = sb("om", [P, P], F32)
        oh = sb("oh", [P, P], F32)
        oc = sb("oc", [P, P], F32)
        ident = sb("ident", [P, P], F32)
        negmax = sb("negmax", [P, 32], F32)
        rowsum = sb("rowsum", [P, 32], F32)
        rowinv = sb("rowinv", [P, 32], F32)
        ps = ctx.enter_context(nc.psum_tensor("ps", [P, 8, 512], F32))

        def flat(buf, first, n):
            return buf[:, first:, :].rearrange("p a n -> p (a n)")[:, 0:n]

        def th(t):
            return slice(t * HALF, (t + 1) * HALF)

        scores = [wraw[:, 0, :], wraw[:, 1, :], flat(tmp, 0, 1024), flat(rt, 0, 1024)]
        table = flat(rt, 2, 1024)
        v_hi = [flat(ah, 0, 2048), flat(al, 0, 2048)]
        v_lo = [flat(wh, 4, 2048), flat(wl, 4, 2048)]
        VEH, VOH, VEL, VOL = (wh[:, k, :] for k in range(4))
        pt_hi = [wl[:, 0, :], wl[:, 2, :]]
        pt_lo = [wl[:, 1, :], wl[:, 3, :]]

        eps_ready = sem("eps_ready")
        x_in = [[sem(f"x_in{t}_{d}") for d in range(4)] for t in range(2)]
        c_in = sem("c_in")
        raw_in = [sem(f"raw_in{r}") for r in range(2)]
        w_hi = [sem(f"w_hi{s}") for s in range(SLOTS)]
        w_lo = [sem(f"w_lo{s}") for s in range(SLOTS)]
        done = [[sem(f"done{s}_{t}") for t in range(2)] for s in range(4)]
        down_last = sem("down_last")
        gbank = [sem(f"gbank{t}") for t in range(2)]
        ubank = [sem(f"ubank{t}") for t in range(2)]
        a_hi = [sem(f"a_hi{t}") for t in range(2)]
        a_lo = [sem(f"a_lo{t}") for t in range(2)]
        down = sem("down")
        dbank = sem("dbank")
        norms = {}
        for ph in ("ffn1", "proj", "ffn2"):
            norms[ph] = {k: sem(f"{ph}_{k}") for k in ("sq", "acc", "stat", "root", "inv", "xn", "hi", "lo0", "lo1")}
        spilled = sem("spilled")
        glu_zero = sem("glu_zero")
        tapc = sem("tapc")
        qk_sq = sem("qk_sq")
        qk_stat = sem("qk_stat")
        qk_rt = sem("qk_rt")
        qk_inv = sem("qk_inv")
        qk_n = sem("qk_n")
        qg_neg = sem("qg_neg")
        v_ready = sem("v_ready")
        v_h = sem("v_h")
        v_l = sem("v_l")
        ln = {k: sem(f"ln_{k}") for k in ("mean", "cent", "sq", "var", "root", "inv", "scaled", "out")}
        tab_in = sem("tab_in")
        v_zero = sem("v_zero")
        vs_in = sem("vs_in")
        st_hi = sem("st_hi")
        st_lo = sem("st_lo")
        st_in = [sem(f"st_in{b}") for b in range(2)]
        carried = sem("carried")
        s_rdy = sem("s_rdy")
        x_rdy = sem("x_rdy")
        p_rdy = sem("p_rdy")
        inv_rdy = sem("inv_rdy")
        pn_rdy = sem("pn_rdy")
        t_rdy = sem("t_rdy")
        pth_rdy = sem("pth_rdy")
        ptl_rdy = sem("ptl_rdy")
        pv_rdy = sem("pv_rdy")
        o_rdy = sem("o_rdy")
        mix_hi = sem("mix_hi")
        mix_lo = sem("mix_lo")
        h_back = sem("h_back")
        wobank = sem("wobank")
        stored = sem("stored")

        def constants_there(eng):
            eng.wait_ge(c_in, 80)

        block = ctx.enter_context(nc.Block())
        NU = 32

        def unit(n):
            return n // 16, (n % 16) // 2, 1 - n % 2

        @block.sync
        def _(sp):
            def load_unit(n, r):
                src = stream[ds(n, 1), :, :].rearrange("a p n -> p (a n)")
                sp.dma_start(wraw[:, r, :], src).then_inc(raw_in[r], 16)

            sp.dma_start(om[:, :], ones_mean).then_inc(c_in, 16)
            sp.dma_start(consts[:, :], smalls).then_inc(c_in, 16)
            for t in range(2):
                for d in range(0, DT, 2):
                    sp.dma_start(h[:, d:d + 2, th(t)], xT[:, d:d + 2, th(t)]).then_inc(x_in[t][d // 2], 16)
                if t == 0:
                    for s in range(2):
                        load_unit(s, s)
            sp.dma_start(oh[:, :], ones_head).then_inc(c_in, 16)
            sp.dma_start(oc[:, :], ones_conv).then_inc(c_in, 16)
            sp.dma_start(ident[:, :], ident_in).then_inc(c_in, 16)
            for s in range(2, 4):
                sp.wait_ge(w_lo[s - 2], 1)
                load_unit(s, s % 2)

            def ffn_loads(ph, first):
                f0, f45 = FILL[ph], FILL45[ph]
                with sp.Fori(0, CHUNKS) as i:
                    for s in (4, 5):
                        sp.wait_ge(w_lo[s - 2], i + (f0 + 1))
                        load_unit(i * 6 + (first + s), s % 2)
                    for s in range(4):
                        if s < 2:
                            sp.wait_ge(w_lo[s + 4], i + (f45 + 1))
                        else:
                            sp.wait_ge(w_lo[s - 2], i + (f0 + 2))
                        load_unit(i * 6 + (first + 6 + s), s % 2)

            def four_loads(ph, steps, first):
                f0 = FILL[ph]
                with sp.Fori(0, steps) as i:
                    for s in range(4):
                        sp.wait_ge(w_lo[(s + 2) % 4], i + (f0 + (1 if s < 2 else 2)))
                        load_unit(i * 4 + (first + 4 + s), s % 2)

            ffn_loads("ffn1", U_FFN1)
            for t in range(2):
                sp.wait_ge(dbank, 4 + 16 * (CHUNKS - 1) + 8 * (t + 1))
                sp.dma_start(h_spill.rearrange("p (d n) -> p d n", d=DT)[:, :, th(t)], h[:, :, th(t)]).then_inc(spilled, 16)
            four_loads("proj", PAIRS, U_PROJ)
            sp.wait_ge(qk_n, 4 + 4 * PAIRS)
            sp.dma_start(table, table_in).then_inc(tab_in, 16)

            sp.wait_ge(v_l, 8)
            sp.wait_ge(v_zero, 4)
            with sp.Fori(0, 2) as it:
                for b in range(2):
                    sp.wait_ge(st_lo, it * 4 + (2 * b + 2))
                    k0 = 4 * b
                    qh, ql, kh = xl[:, k0, :], xl[:, k0 + 1, :], xl[:, k0 + 2, :]
                    lo, hi = slice(0, DH), slice(DH, P)
                    for dst, src in (
                        (xh[lo, k0, :], qh[lo, :]), (xh[hi, k0, :], ql[lo, :]),
                        (xh[hi, k0 + 1, :], qh[hi, :]), (xh[lo, k0 + 1, :], ql[hi, :]),
                        (xh[lo, k0 + 2, :], kh[lo, :]), (xh[hi, k0 + 2, :], kh[lo, :]),
                        (xh[lo, k0 + 3, :], kh[hi, :]), (xh[hi, k0 + 3, :], kh[hi, :]),
                    ):
                        sp.dma_start(dst.bitcast(F32), src.bitcast(F32)).then_inc(st_in[b], 16)
                for b in range(2):
                    sp.wait_ge(pv_rdy, it * NU + (16 * b + 1))
                    for e, (dh, dl) in enumerate(((VEH, VEL), (VOH, VOL))):
                        for k, (dst, src) in enumerate(((dh, v_hi), (dl, v_lo))):
                            for q in range(2):
                                sp.dma_start(
                                    dst.bitcast(F32).rearrange("p (t c) -> p t c", c=P)[:, 4 * q:4 * q + 4, DH * e:DH * e + DH],
                                    src[q].bitcast(F32).rearrange("p (t c) -> p t c", c=HALF)[:, :, ds(it * (2 * P) + (b * P + e * DH), DH)],
                                ).then_inc(vs_in, 16)
            for d in range(DT):
                sp.wait_ge(mix_lo, 8)
                sp.dma_start(h[:, d, :], h_spill[:, d * SEQ:(d + 1) * SEQ]).then_inc(h_back, 16)
            four_loads("wo", 2, U_WO)
            ffn_loads("ffn2", U_FFN2)
            for q in range(16):
                t, d = q // 8, q % 8
                sp.wait_ge(dbank, 4 + DUSE["ffn2"] + 16 * (CHUNKS - 1) + q + 1)
                sp.dma_start(outT[:, d, th(t)], h[:, d, th(t)]).then_inc(stored, 16)
            sp.wait_ge(stored, 256)

        @block.gpsimd
        def _(pool):
            pool.memset(glu[:, 0:TAPS - 1], 0.0).then_inc(glu_zero, 1)

            def norm_sums(ph):
                m = norms[ph]
                for t in range(2):
                    acc = rt[:, 2 + t, :]
                    for d in range(1, DT):
                        pool.wait_ge(m["sq"], 8 * t + d + 1)
                        if d == 1:
                            pool.tensor_tensor(acc, tmp[:, 0, :], tmp[:, 1, :], ALU.add).then_inc(m["acc"], 1)
                        else:
                            pool.wait_ge(m["acc"], 7 * t + d - 1)
                            pool.tensor_tensor(acc, acc, tmp[:, d % 2, :], ALU.add).then_inc(m["acc"], 1)

            norm_sums("ffn1")
            norm_sums("proj")
            pool.wait_ge(done[3][1], FILL["v"] + 1)
            pool.memset(VEH.bitcast(F32).rearrange("p (t c) -> p t c", c=P)[:, :, DH:P], 0.0).then_inc(v_zero, 1)
            pool.memset(VOH.bitcast(F32).rearrange("p (t c) -> p t c", c=P)[:, :, 0:DH], 0.0).then_inc(v_zero, 1)
            pool.memset(VEL.bitcast(F32).rearrange("p (t c) -> p t c", c=P)[:, :, DH:P], 0.0).then_inc(v_zero, 1)
            pool.memset(VOL.bitcast(F32).rearrange("p (t c) -> p t c", c=P)[:, :, 0:DH], 0.0).then_inc(v_zero, 1)
            norm_sums("ffn2")

        @block.scalar
        def _(act):
            def norm_squares(ph):
                m = norms[ph]
                for t in range(2):
                    for d in range(DT):
                        if ph == "ffn1":
                            act.wait_ge(x_in[t][d // 2], 16)
                        elif ph == "proj":
                            act.wait_ge(dbank, 4 + 16 * (CHUNKS - 1) + 8 * t + d + 1)
                        else:
                            act.wait_ge(wobank, 4 + 2 * d + t + 1)
                        q = 8 * t + d
                        if q >= 2:
                            act.wait_ge(m["acc"], 7 * t + d - 2 if d > 2 else (7 * t + 1 if d == 2 else 7 * t))
                        nc.scalar.activation(tmp[:, d % 2, :], h[:, d, th(t)], ACT.Square).then_inc(m["sq"], 1)

            def norm_rest(ph):
                m = norms[ph]
                for t in range(2):
                    act.wait_ge(m["stat"], t + 1)
                    nc.scalar.activation(rt[:, t, :], ps[:, 2 * t, :], ACT.Sqrt, bias=eps_col[:, 0:1]).then_inc(m["root"], 1)
                for t in range(2):
                    for d in range(DT):
                        act.wait_ge(m["xn"], 8 * t + d + 1)
                        nc.scalar.activation(xh[:, d, th(t)], tmp[:, 2 + d % 2, :], ACT.Copy).then_inc(m["hi"], 1)

            def ffn(ph):
                f0, f45, b0 = FILL[ph], FILL45[ph], BANKUSE[ph]
                u0 = {"ffn1": U_FFN1, "ffn2": U_FFN2}[ph]
                with act.Fori(0, CHUNKS) as i:
                    for f in range(2):
                        for t in range(2):
                            n = 2 * f + t
                            act.wait_ge(done[2 * f][t], i + (f0 + 1))
                            act.wait_ge(ubank[t], i * 2 + (b0 + f + 1))
                            nc.scalar.activation(tmp[:, t, :], ps[:, 2 * t, :], ACT.Silu).then_inc(gbank[t], 1)
                            if n == 0:
                                for s in (4, 5):
                                    act.wait_ge(down_last, i + (f45 + 1))
                                    act.wait_ge(raw_in[s % 2], i * 48 + 16 * ((u0 + s) // 2 + 1))
                                    nc.scalar.activation(wh[:, s, :], wraw[:, s % 2, :], ACT.Copy).then_inc(w_hi[s], 1)
                            act.wait_ge(ubank[t], i * 2 + (b0 + f + 2))
                            nc.scalar.activation(ah[:, f, th(t)], tmp[:, 2 + t, :], ACT.Copy).then_inc(a_hi[t], 1)
                            if t == 1:
                                for s in (2 * f, 2 * f + 1):
                                    act.wait_ge(done[s][1], i + (f0 + 1))
                                    act.wait_ge(raw_in[s % 2], i * 48 + 16 * ((u0 + 6 + s) // 2 + 1))
                                    nc.scalar.activation(wh[:, s, :], wraw[:, s % 2, :], ACT.Copy).then_inc(w_hi[s], 1)

            act.sem_inc(down_last, 1)
            for t in range(2):
                act.sem_inc(ubank[t], 1)
            act.wait_ge(eps_ready, 2)
            norm_squares("ffn1")
            for s in range(4):
                act.wait_ge(raw_in[s % 2], 16 * (s // 2 + 1))
                nc.scalar.activation(wh[:, s, :], wraw[:, s % 2, :], ACT.Copy).then_inc(w_hi[s], 1)
            norm_rest("ffn1")
            ffn("ffn1")
            norm_squares("proj")
            norm_rest("proj")

            f0, b0 = FILL["proj"], BANKUSE["proj"]
            act.wait_ge(spilled, 32)
            with act.Fori(0, PAIRS) as i:
                for t in range(2):
                    act.wait_ge(done[0][t], i + (f0 + 1))
                    act.wait_ge(ubank[t], i * 2 + (b0 + 1))
                    nc.scalar.activation(tmp[:, t, :], ps[:, 2 * t, :], ACT.Sigmoid).then_inc(gbank[t], 1)
                for s in (0, 1):
                    act.wait_ge(done[s][1], i + (f0 + 1))
                    act.wait_ge(raw_in[s % 2], i * 32 + 16 * ((U_PROJ + 4 + s) // 2 + 1))
                    nc.scalar.activation(wh[:, s, :], wraw[:, s % 2, :], ACT.Copy).then_inc(w_hi[s], 1)
                for t in range(2):
                    constants_there(act)
                    act.wait_ge(done[2][t], i + (f0 + 1))
                    act.wait_ge(ubank[t], i * 2 + (b0 + 2))
                    nc.scalar.activation(h[:, ds(i * 2, 1), th(t)].rearrange("p a n -> p (a n)"), ps[:, 2 * t, :], ACT.Copy).then_inc(qk_sq, 1)
                    nc.scalar.activation(tmp[:, t, :], ps[:, 2 * t, :], ACT.Square).then_inc(gbank[t], 1)
                    constants_there(act)
                    act.wait_ge(done[3][t], i + (f0 + 1))
                    nc.scalar.activation(h[:, ds(i * 2 + 1, 1), th(t)].rearrange("p a n -> p (a n)"), ps[:, 2 * t + 1, :], ACT.Copy).then_inc(qk_sq, 1)
                    nc.scalar.activation(tmp[:, 2 + t, :], ps[:, 2 * t + 1, :], ACT.Square).then_inc(ubank[t], 1)
                for s in (2, 3):
                    act.wait_ge(done[s][1], i + (f0 + 1))
                    act.wait_ge(raw_in[s % 2], i * 32 + 16 * ((U_PROJ + 4 + s) // 2 + 1))
                    nc.scalar.activation(wh[:, s, :], wraw[:, s % 2, :], ACT.Copy).then_inc(w_hi[s], 1)
                for n in range(4):
                    act.wait_ge(qk_stat, i * 4 + (n + 1))
                    act.wait_ge(qk_n, i * 4 + (n + 1))
                    if n % 2 == 0:
                        nc.scalar.activation(rt[:, n, :], ps[:, 4 + n, :], ACT.Sqrt, scale=64.0, bias=eps_col[:, 1:2]).then_inc(qk_rt, 1)
                    else:
                        nc.scalar.activation(rt[:, n, :], ps[:, 4 + n, :], ACT.Sqrt, bias=eps_col[:, 0:1]).then_inc(qk_rt, 1)

            for tt in range(8):
                if tt in (3, 7):
                    act.wait_ge(done[3][tt // 4], FILL["v"] + 1)
                else:
                    act.wait_ge(v_ready, tt + 1 - (tt > 3))
                nc.scalar.activation(v_hi[tt // 4][:, (tt % 4) * 512:(tt % 4 + 1) * 512], ps[:, 4 + tt % 4, :], ACT.Copy).then_inc(v_h, 1)

            for t in range(2):
                for k in range(4):
                    act.wait_ge(ln["cent"], 4 * t + k + 1)
                    q = 4 * t + k
                    if q >= 2:
                        act.wait_ge(ln["var"], q - 1)
                    nc.scalar.activation(tmp[:, 2 + k % 2, :], y[:, k, th(t)], ACT.Square).then_inc(ln["sq"], 1)
            for t in range(2):
                act.wait_ge(ln["var"], 4 * t + 4)
                act.wait_ge(ln["cent"], 8)
                nc.scalar.activation(tmp[:, t, :], ps[:, 2 + t, :], ACT.Sqrt, bias=eps_col[:, 0:1]).then_inc(ln["root"], 1)
            for t in range(2):
                for k in range(4):
                    act.wait_ge(ln["scaled"], 4 * t + k + 1)
                    nc.scalar.activation(y[:, k, th(t)], y[:, k, th(t)], ACT.Silu, bias=consts[:, C_LB + k:C_LB + k + 1]).then_inc(ln["out"], 1)

            act.wait_ge(qk_n, 4 + 4 * PAIRS)
            act.wait_ge(ln["out"], 8)
            act.wait_ge(done[3][1], FILL["v"] + 1)
            with act.Fori(0, 2) as it:
                for b in range(2):
                    for which, dst in ((0, 0), (1, 2)):
                        src = h[:, ds(it * 4 + (2 * b + which), 1), :].rearrange("p a n -> p (a n)")
                        nc.scalar.activation(xl[:, 4 * b + dst, :], src, ACT.Copy).then_inc(st_hi, 1)

                def probs_hi(n):
                    b, i, e = unit(n)
                    nk = (i + 1) * P
                    act.wait_ge(t_rdy, it * NU + (n + 1))
                    if n >= 2:
                        act.wait_ge(pv_rdy, it * NU + n)
                    nc.scalar.activation(pt_hi[n % 2][:, 0:nk], flat(ps, 4, nk), ACT.Copy).then_inc(pth_rdy, 1)

                def head_out(n):
                    b, i, e = unit(n)
                    m = n // 2
                    constants_there(act)
                    act.wait_ge(pv_rdy, it * NU + (n + 2))
                    dst = h[:, ds(it * 4 + 2 * b, 1), i * P:(i + 1) * P].rearrange("p a n -> p (a n)")
                    nc.scalar.activation(dst, ps[:, 6 + m % 2, 0:P], ACT.Copy).then_inc(o_rdy, 1)

                for n in range(NU + 2):
                    if n < NU:
                        b, i, e = unit(n)
                        nk = (i + 1) * P
                        act.wait_ge(x_rdy, it * NU + (n + 1))
                        nc.scalar.activation(scores[n % 4][:, 0:nk], scores[n % 4][:, 0:nk], ACT.Exp, bias=negmax[:, n:n + 1],
                                             scale=-1.0, accum_out=rowsum[:, n:n + 1]).then_inc(p_rdy, 1)
                    if 1 <= n <= NU:
                        probs_hi(n - 1)
                    if n >= 2 and (n - 2) % 2 == 1:
                        head_out(n - 2)

            act.wait_ge(ptl_rdy, 2 * NU)
            act.wait_ge(pv_rdy, 2 * NU + 1)
            for s in range(2):
                act.dma_start(wraw[:, s, :], stream[U_WO + s, :, :]).then_inc(raw_in[s], 16)

            def wo_unit(s):
                act.wait_ge(raw_in[s % 2], 16 * ((U_WO + s) // 2 + 1))
                nc.scalar.activation(wh[:, s, :], wraw[:, s % 2, :], ACT.Copy).then_inc(w_hi[s], 1)

            def mix(m):
                act.wait_ge(o_rdy, 32)
                src = h[:, 2 * m, :] if m < 4 else y[:, m - 4, :]
                nc.scalar.activation(xh[:, m, :], src, ACT.Copy).then_inc(mix_hi, 1)

            for m in range(DT):
                if m == 2:
                    wo_unit(0)
                    wo_unit(1)
                mix(m)
            for s in (2, 3):
                act.wait_ge(w_lo[s - 2], FILL["wo"] + 1)
                act.dma_start(wraw[:, s % 2, :], stream[U_WO + s, :, :]).then_inc(raw_in[s % 2], 16)
                wo_unit(s)
            f0 = FILL["wo"]
            with act.Fori(0, 2) as i:
                for s in range(4):
                    act.wait_ge(done[s][1], i + (f0 + 1))
                    act.wait_ge(raw_in[s % 2], i * 32 + 16 * ((U_WO + 4 + s) // 2 + 1))
                    nc.scalar.activation(wh[:, s, :], wraw[:, s % 2, :], ACT.Copy).then_inc(w_hi[s], 1)
            norm_squares("ffn2")
            norm_rest("ffn2")
            ffn("ffn2")

        @block.vector
        def _(dve):
            def lo_part(s, value):
                dve.wait_ge(w_hi[s], value)
                nc.vector.tensor_tensor(wl[:, s, :], wraw[:, s % 2, :], wh[:, s, :].bitcast(F32), ALU.subtract).then_inc(w_lo[s], 1)

            def norm(ph):
                m = norms[ph]
                for t in range(2):
                    dve.wait_ge(m["root"], t + 1)
                    nc.vector.reciprocal(rt[:, t, :], rt[:, t, :]).then_inc(m["inv"], 1)
                    for d in range(DT):
                        q = 8 * t + d
                        dve.wait_ge(m["inv"], t + 1)
                        g = C_G[ph] + d
                        nc.vector.scalar_tensor_tensor(out=tmp[:, 2 + d % 2, :], in0=h[:, d, th(t)], scalar=consts[:, g:g + 1],
                                                       in1=rt[:, t, :], op0=ALU.mult, op1=ALU.mult).then_inc(m["xn"], 1)
                        dve.wait_ge(m["hi"], q + 1)
                        nc.vector.tensor_tensor(xl[:, d, th(t)], tmp[:, 2 + d % 2, :], xh[:, d, th(t)].bitcast(F32),
                                                ALU.subtract).then_inc(m[f"lo{t}"], 1)

            def ffn(ph):
                f0, f45, b0, d0 = FILL[ph], FILL45[ph], BANKUSE[ph], DUSE[ph]
                with dve.Fori(0, CHUNKS) as i:
                    def gated(f, t):
                        dve.wait_ge(gbank[t], i * 2 + (b0 + f + 2))
                        dve.wait_ge(done[2 * f + 1][t], i + (f0 + 1))
                        nc.vector.tensor_tensor(tmp[:, 2 + t, :], tmp[:, t, :], ps[:, 2 * t + 1, :], ALU.mult).then_inc(ubank[t], 1)
                        dve.wait_ge(a_hi[t], i * 2 + (b_ffn + f + 1))
                        nc.vector.tensor_tensor(al[:, f, th(t)], tmp[:, 2 + t, :], ah[:, f, th(t)].bitcast(F32),
                                                ALU.subtract).then_inc(a_lo[t], 1)

                    def add_down(q):
                        t, d = q // 8, q % 8
                        if q == 15:
                            dve.wait_ge(down_last, i + (f45 + 2))
                        else:
                            dve.wait_ge(down, i * 15 + (15 * d0 // 16 + q + 1))
                        nc.vector.scalar_tensor_tensor(out=h[:, d, th(t)], in0=ps[:, 4 + q % 4, :], scalar=0.5,
                                                       in1=h[:, d, th(t)], op0=ALU.mult, op1=ALU.add).then_inc(dbank, 1)

                    b_ffn = {"ffn1": 0, "ffn2": 2 * CHUNKS}[ph]
                    gated(0, 0)
                    lo_part(4, i + (f45 + 1))
                    lo_part(5, i + (f45 + 1))
                    gated(0, 1)
                    lo_part(0, i + (f0 + 2))
                    lo_part(1, i + (f0 + 2))
                    gated(1, 0)
                    gated(1, 1)
                    for q in range(16):
                        add_down(q)
                        if q == 3:
                            lo_part(2, i + (f0 + 2))
                            lo_part(3, i + (f0 + 2))

            nc.vector.memset(eps_col[:, 0:1], EPS).then_inc(eps_ready, 1)
            nc.vector.memset(eps_col[:, 1:2], 64 * EPS).then_inc(eps_ready, 1)
            dve.sem_inc(qk_n, 4)
            dve.wait_ge(c_in, 80)
            nc.vector.tensor_scalar(negqg[:, :], consts[:, C_QG:C_QG + 1], -1.0, None, ALU.mult).then_inc(qg_neg, 1)
            for s in range(4):
                lo_part(s, 1)
            norm("ffn1")
            ffn("ffn1")
            norm("proj")

            f0, b0 = FILL["proj"], BANKUSE["proj"]
            dve.wait_ge(qg_neg, 1)
            dve.wait_ge(glu_zero, 1)
            with dve.Fori(0, PAIRS) as i:
                for t in range(2):
                    dve.wait_ge(gbank[t], i * 2 + (b0 + 2))
                    dve.wait_ge(done[1][t], i + (f0 + 1))
                    nc.vector.tensor_tensor(glu[:, TAPS - 1 + t * HALF:TAPS - 1 + (t + 1) * HALF], tmp[:, t, :], ps[:, 2 * t + 1, :],
                                            ALU.mult).then_inc(ubank[t], 1)
                lo_part(0, i + (f0 + 2))
                lo_part(1, i + (f0 + 2))
                ytile = y[:, ds(i, 1), :].rearrange("p a n -> p (a n)")
                for k in range(TAPS):
                    if k == 0:
                        dve.wait_ge(ubank[1], i * 2 + (b0 + 2))
                        nc.vector.tensor_scalar(ytile, glu[:, 0:SEQ], consts[:, ds(i * TAPS + C_CW, 1)], consts[:, ds(i + C_CB, 1)],
                                                ALU.mult, ALU.add).then_inc(tapc, 1)
                    else:
                        dve.wait_ge(tapc, i * TAPS + k)
                        nc.vector.scalar_tensor_tensor(out=ytile, in0=glu[:, k:k + SEQ], scalar=consts[:, ds(i * TAPS + (C_CW + k), 1)],
                                                       in1=ytile, op0=ALU.mult, op1=ALU.add).then_inc(tapc, 1)
                    if k == 18:
                        lo_part(2, i + (f0 + 2))
                        lo_part(3, i + (f0 + 2))
                for n in range(4):
                    t, which = n // 2, n % 2
                    dve.wait_ge(qk_rt, i * 4 + (n + 1))
                    nc.vector.reciprocal(rt[:, n, :], rt[:, n, :]).then_inc(qk_inv, 1)
                for n in range(4):
                    t, which = n // 2, n % 2
                    dve.wait_ge(qk_inv, i * 4 + (n + 1))
                    tile = h[:, ds(i * 2 + which, 1), th(t)].rearrange("p a n -> p (a n)")
                    gain = consts[:, C_KG:C_KG + 1] if which else negqg[:, 0:1]
                    nc.vector.scalar_tensor_tensor(out=tile, in0=tile, scalar=gain, in1=rt[:, n, :], op0=ALU.mult,
                                                   op1=ALU.mult).then_inc(qk_n, 1)

            for tt in range(8):
                dve.wait_ge(v_h, tt + 1)
                c = slice((tt % 4) * 512, (tt % 4 + 1) * 512)
                nc.vector.tensor_tensor(v_lo[tt // 4][:, c], ps[:, 4 + tt % 4, :], v_hi[tt // 4][:, c].bitcast(F32),
                                        ALU.subtract).then_inc(v_l, 1)

            for t in range(2):
                dve.wait_ge(ln["mean"], t + 1)
                for k in range(4):
                    nc.vector.tensor_tensor(y[:, k, th(t)], y[:, k, th(t)], ps[:, t, :], ALU.subtract).then_inc(ln["cent"], 1)
            for t in range(2):
                dve.wait_ge(ln["root"], t + 1)
                nc.vector.reciprocal(tmp[:, t, :], tmp[:, t, :]).then_inc(ln["inv"], 1)
                dve.wait_ge(ln["inv"], t + 1)
                dve.wait_ge(ln["sq"], 8)
                for k in range(4):
                    nc.vector.scalar_tensor_tensor(out=y[:, k, th(t)], in0=y[:, k, th(t)], scalar=consts[:, C_LG + k:C_LG + k + 1],
                                                   in1=tmp[:, t, :], op0=ALU.mult, op1=ALU.mult).then_inc(ln["scaled"], 1)

            dve.wait_ge(tab_in, 16)
            with dve.Fori(0, 2) as it:
                for b in range(2):
                    for which, hi_at, lo_at in ((0, 0, 1), (1, 2, 3)):
                        dve.wait_ge(st_hi, it * 4 + (2 * b + which + 1))
                        src = h[:, ds(it * 4 + (2 * b + which), 1), :].rearrange("p a n -> p (a n)")
                        nc.vector.tensor_tensor(xl[:, 4 * b + lo_at, :], src, xl[:, 4 * b + hi_at, :].bitcast(F32),
                                                ALU.subtract).then_inc(st_lo, 1)

                def masked(n):
                    b, i, e = unit(n)
                    nk = (i + 1) * P
                    if n < 3:
                        dve.wait_ge(s_rdy, it * NU + (n + 1))
                        nc.vector.memset(rowinv[:, n:n + 1], 0.0).then_inc(carried, 1)
                    nc.vector.tensor_tensor_reduce(scores[n % 4][:, 0:nk], flat(ps, 2 * (n % 2), nk), table[:, SEQ - nk:SEQ], 1.0, 3e38,
                                                   ALU.add, ALU.min, negmax[:, n:n + 1]).then_inc(x_rdy, 1)

                def normalised(n):
                    b, i, e = unit(n)
                    nk = (i + 1) * P
                    dve.wait_ge(p_rdy, it * NU + (n + 1))
                    nc.vector.reciprocal(rowinv[:, n:n + 1], rowsum[:, n:n + 1]).then_inc(inv_rdy, 1)
                    dve.wait_ge(inv_rdy, it * NU + (n + 1))
                    nc.vector.tensor_scalar(scores[n % 4][:, 0:nk], scores[n % 4][:, 0:nk], rowinv[:, n:n + 1], None,
                                            ALU.mult).then_inc(pn_rdy, 1)

                def probs_lo(n):
                    b, i, e = unit(n)
                    nk = (i + 1) * P
                    dve.wait_ge(pth_rdy, it * NU + (n + 1))
                    if n + 3 < NU:
                        dve.wait_ge(s_rdy, it * NU + (n + 4))
                    nc.vector.tensor_tensor(pt_lo[n % 2][:, 0:nk], flat(ps, 4, nk), pt_hi[n % 2][:, 0:nk].bitcast(F32),
                                            ALU.subtract).then_inc(ptl_rdy, 1)

                for n in range(NU + 2):
                    if n < NU:
                        masked(n)
                    if 1 <= n <= NU:
                        normalised(n - 1)
                    if n >= 2:
                        probs_lo(n - 2)

            def mix(m):
                dve.wait_ge(mix_hi, m + 1)
                src = h[:, 2 * m, :] if m < 4 else y[:, m - 4, :]
                nc.vector.tensor_tensor(xl[:, m, :], src, xh[:, m, :].bitcast(F32), ALU.subtract).then_inc(mix_lo, 1)

            f0 = FILL["wo"]
            for m in range(DT):
                if m == 2:
                    lo_part(0, f0 + 1)
                    lo_part(1, f0 + 1)
                mix(m)
            for s in (2, 3):
                lo_part(s, f0 + 1)
            with dve.Fori(0, 2) as i:
                for s in range(4):
                    for t in range(2):
                        dve.wait_ge(done[s][t], i + (f0 + 1))
                        dve.wait_ge(h_back, 16 * DT)
                        tile = h[:, ds(i * 4 + s, 1), th(t)].rearrange("p a n -> p (a n)")
                        nc.vector.tensor_tensor(tile, ps[:, 4 + (2 * s + t) % 4, :], tile, ALU.add).then_inc(wobank, 1)
                    lo_part(s, i + (f0 + 2))
            norm("ffn2")
            ffn("ffn2")

        @block.tensor
        def _(pe):
            def three(out, lhs_hi, lhs_lo, rhs_hi, rhs_lo, start, stop):
                nc.tensor.matmul(out, lhs_hi, rhs_hi, start=start, stop=False)
                nc.tensor.matmul(out, lhs_hi, rhs_lo, start=False, stop=False)
                return nc.tensor.matmul(out, lhs_lo, rhs_hi, start=False, stop=stop)

            def norm_stats(ph):
                m = norms[ph]
                for t in range(2):
                    pe.wait_ge(m["acc"], 7 * (t + 1))
                    nc.tensor.matmul(ps[:, 2 * t, :], om[:, :], rt[:, 2 + t, :], start=True, stop=True).then_inc(m["stat"], 1)

            def column(bank, s, t, ready=None):
                for d in range(DT):
                    if ready is not None:
                        pe.wait_ge(ready, d + 1)
                    c = slice(d * P, (d + 1) * P)
                    mm = three(ps[:, bank, :], wh[:, s, c], wl[:, s, c], xh[:, d, th(t)], xl[:, d, th(t)], d == 0, d == DT - 1)
                return mm

            def ffn(ph):
                f0, f45, b0, d0 = FILL[ph], FILL45[ph], BANKUSE[ph], DUSE[ph]
                b_ffn = {"ffn1": 0, "ffn2": 2 * CHUNKS}[ph]
                with pe.Fori(0, CHUNKS) as i:
                    for f in range(2):
                        for t in range(2):
                            ready = norms[ph][f"lo{t}"] if f == 0 else None
                            pe.wait_ge(gbank[t], i * 2 + (b0 + f + 1))
                            if t == 0:
                                pe.wait_ge(w_lo[2 * f], i + (f0 + 1))
                            column(2 * t, 2 * f, t, ready).then_inc(done[2 * f][t], 1)
                            pe.wait_ge(ubank[t], i * 2 + (b0 + f + 1))
                            if t == 0:
                                pe.wait_ge(w_lo[2 * f + 1], i + (f0 + 1))
                            column(2 * t + 1, 2 * f + 1, t).then_inc(done[2 * f + 1][t], 1)
                    for q in range(16):
                        t, d = q // 8, q % 8
                        if q == 0:
                            pe.wait_ge(w_lo[4], i + (f45 + 1))
                            pe.wait_ge(w_lo[5], i + (f45 + 1))
                        if d == 0:
                            pe.wait_ge(a_lo[t], i * 2 + (b_ffn + 2))
                        pe.wait_ge(dbank, i * 16 + (d0 + q + 1))
                        c = slice(d * P, (d + 1) * P)
                        for f in range(2):
                            mm = three(ps[:, 4 + q % 4, :], wh[:, 4 + f, c], wl[:, 4 + f, c], ah[:, f, th(t)], al[:, f, th(t)], f == 0, f == 1)
                        mm.then_inc(down_last if q == 15 else down, 1)

            for t in range(2):
                pe.sem_inc(gbank[t], 1)
            pe.sem_inc(dbank, 4)
            pe.sem_inc(wobank, 4)
            pe.sem_inc(pv_rdy, 1)
            pe.wait_ge(c_in, 80)
            norm_stats("ffn1")
            ffn("ffn1")
            norm_stats("proj")
            f0, b0 = FILL["proj"], BANKUSE["proj"]
            with pe.Fori(0, PAIRS) as i:
                for part in range(2):
                    for t in range(2):
                        ready = norms["proj"][f"lo{t}"] if part == 0 else None
                        pe.wait_ge(gbank[t], i * 2 + (b0 + part + 1))
                        if t == 0:
                            pe.wait_ge(w_lo[2 * part], i + (f0 + 1))
                        column(2 * t, 2 * part, t, ready).then_inc(done[2 * part][t], 1)
                        pe.wait_ge(ubank[t], i * 2 + (b0 + part + 1))
                        if t == 0:
                            pe.wait_ge(w_lo[2 * part + 1], i + (f0 + 1))
                        column(2 * t + 1, 2 * part + 1, t).then_inc(done[2 * part + 1][t], 1)
                for n in range(4):
                    t, which = n // 2, n % 2
                    pe.wait_ge((ubank if which else gbank)[t], i * 2 + (b0 + 3))
                    nc.tensor.matmul(ps[:, 4 + n, :], oh[:, :], tmp[:, 2 * which + t, :], start=True, stop=True).then_inc(qk_stat, 1)

            pe.wait_ge(qk_rt, 4 * PAIRS)
            for tt in range(8):
                if tt >= 4:
                    pe.wait_ge(v_l, tt - 3)
                for d in range(DT):
                    s, r = d // 2, d % 2
                    if tt == 0 and r == 0:
                        pe.wait_ge(w_lo[s], FILL["v"] + 1)
                    c = slice(tt * P, (tt + 1) * P)
                    w = slice(r * 512, (r + 1) * 512)
                    mm = three(ps[:, 4 + tt % 4, :], xh[:, d, c], xl[:, d, c], wh[:, s, w], wl[:, s, w], d == 0, d == DT - 1)
                    if tt in (3, 7) and r == 1:
                        mm.then_inc(done[s][tt // 4], 1)
                if tt not in (3, 7):
                    mm.then_inc(v_ready, 1)

            pe.wait_ge(tapc, PAIRS * TAPS)
            for t in range(2):
                for k in range(4):
                    mm = nc.tensor.matmul(ps[:, t, :], oc[:, :], y[:, k, th(t)], start=(k == 0), stop=(k == 3))
                mm.then_inc(ln["mean"], 1)
            for t in range(2):
                for k in range(4):
                    pe.wait_ge(ln["sq"], 4 * t + k + 1)
                    nc.tensor.matmul(ps[:, 2 + t, :], oc[:, :], tmp[:, 2 + k % 2, :], start=(k == 0), stop=(k == 3)).then_inc(ln["var"], 1)

            pe.wait_ge(ln["root"], 2)
            with pe.Fori(0, 2) as it:
                def score(n):
                    b, i, e = unit(n)
                    if n % 16 == 0:
                        pe.wait_ge(st_in[b], it * 128 + 128)
                    if n >= 2:
                        pe.wait_ge(x_rdy, it * NU + (n - 1))
                    nk = (i + 1) * P
                    rows = slice(DH * e, DH * e + DH)
                    q = slice(i * P, (i + 1) * P)
                    for c in range(0, nk, 512):
                        w = min(512, nk - c)
                        out = ps[:, 2 * (n % 2) + c // 512, 0:w]
                        nc.tensor.matmul(out, xh[:, 4 * b + e, q], xh[:, 4 * b + 2 + e, c:c + w], start=True, stop=False)
                        mm = nc.tensor.matmul(out, xl[rows, 4 * b, q], xl[rows, 4 * b + 3, c:c + w], start=False, stop=True)
                    mm.then_inc(s_rdy, 1)

                def turn(n):
                    b, i, e = unit(n)
                    pe.wait_ge(pn_rdy, it * NU + (n + 1))
                    if n >= 1:
                        pe.wait_ge(ptl_rdy, it * NU + n)
                    for j in range(i + 1):
                        mm = nc.tensor.transpose(ps[:, 4 + j // 4, (j % 4) * P:(j % 4 + 1) * P], scores[n % 4][:, j * P:(j + 1) * P],
                                                 ident[:, :])
                    mm.then_inc(t_rdy, 1)

                def weighted(n):
                    b, i, e = unit(n)
                    m = n // 2
                    if n % 16 == 0:
                        pe.wait_ge(vs_in, it * 256 + 128 * (b + 1))
                    pe.wait_ge(ptl_rdy, it * NU + (n + 1))
                    if e == 1 and m >= 2:
                        pe.wait_ge(o_rdy, it * 16 + (m - 1))
                    vh, vl = (VOH, VOL) if e else (VEH, VEL)
                    for j in range(i + 1):
                        c = slice(j * P, (j + 1) * P)
                        mm = three(ps[:, 6 + m % 2, 0:P], vh[:, c], vl[:, c], pt_hi[n % 2][:, c], pt_lo[n % 2][:, c],
                                   e == 1 and j == 0, e == 0 and j == i)
                    mm.then_inc(pv_rdy, 1)

                score(0)
                for n in range(NU + 2):
                    if n + 1 < NU:
                        score(n + 1)
                    if 1 <= n <= NU:
                        turn(n - 1)
                    if n >= 2:
                        weighted(n - 2)

            f0 = FILL["wo"]
            pe.wait_ge(o_rdy, 32)
            with pe.Fori(0, 2) as i:
                for s in range(4):
                    pe.wait_ge(w_lo[s], i + (f0 + 1))
                    for t in range(2):
                        pe.wait_ge(wobank, i * 8 + (2 * s + t + 1))
                        ready = mix_lo if s == 0 and t == 0 else None
                        column(4 + (2 * s + t) % 4, s, t, ready).then_inc(done[s][t], 1)
            norm_stats("ffn2")
            ffn("ffn2")


def kernel(**inputs):
    import numpy as np
    import concourse.bacc as bacc
    from concourse.bass_utils import run_bass_kernel_spmd

    w = {k: np.asarray(v) for k, v in inputs.items()}

    def columns(m):
        return m.reshape(DT, P, -1, P).transpose(2, 1, 0, 3).reshape(-1, P, UNIT)

    def ffn_units(gate, up, down):
        g, u, d = columns(gate), columns(up), down.reshape(FT, P, UNIT)
        return [x for c in range(CHUNKS) for x in (g[2 * c], u[2 * c], g[2 * c + 1], u[2 * c + 1], d[2 * c], d[2 * c + 1])]

    w_in = columns(w["w_in"][0])
    v_units = w["w_in"][0][:, 1024:1536].reshape(4, 2, P, 512).transpose(0, 2, 1, 3).reshape(4, P, UNIT)
    units = ffn_units(w["ffn1_w_gate"][0], w["ffn1_w_up"][0], w["ffn1_w_down"][0])
    for p in range(PAIRS):
        units += [w_in[16 + p], w_in[12 + p], w_in[p], w_in[4 + p]]
    units += list(v_units)
    units += list(columns(w["w_out"][0]))
    units += ffn_units(w["ffn2_w_gate"][0], w["ffn2_w_up"][0], w["ffn2_w_down"][0])
    units += [np.zeros((P, UNIT), np.float32)] * 4

    def tiles(v):
        return v.reshape(-1, P).T

    smalls = np.concatenate([
        tiles(w["ffn1_norm"][0]), tiles(w["mix_norm"][0]), tiles(w["ffn2_norm"][0]),
        w["conv_w"][0].reshape(TAPS, 4, P).transpose(2, 1, 0).reshape(P, 4 * TAPS),
        tiles(w["conv_b"][0]), tiles(w["conv_ln_g"][0]), tiles(w["conv_ln_b"][0]),
        np.tile(w["q_norm"][0], 2)[:, None], np.tile(w["k_norm"][0], 2)[:, None]], axis=1)

    head = np.arange(P) // DH
    same_head = np.where(head[:, None] == head[None, :], 1.0 / DH, 0.0).astype(np.float32)
    dist = np.arange(P)[:, None] + (SEQ - P) - np.arange(SEQ)[None, :]
    count = sum(((dist >= 0) & (dist <= window) & (dist % step == 0)).astype(int)
                for window, step in ((128, 1), (512, 4), (2048, 16)))
    table = np.where(count > 0, -np.log(np.maximum(count, 1)), -NEG).astype(np.float32)

    arrays = {
        "xT": w["x"][0].T.reshape(DT, P, SEQ).transpose(1, 0, 2),
        "stream": np.stack(units),
        "smalls": smalls,
        "ones_mean": np.full((P, P), 1.0 / D, np.float32),
        "ones_head": same_head,
        "ones_conv": np.full((P, P), 1.0 / 512, np.float32),
        "ident": np.eye(P, dtype=np.float32),
        "table": table,
    }
    arrays = {f"in_{k}": np.ascontiguousarray(v) for k, v in arrays.items()}
    nc = bacc.Bacc("TRN2", target_bir_lowering=False, num_devices=1)
    args = [nc.dram_tensor(k, a.shape, mybir.dt.from_np(a.dtype), kind="ExternalInput").ap() for k, a in arrays.items()]
    args.append(nc.dram_tensor("outT", (P, DT, SEQ), F32, kind="ExternalOutput").ap())
    build(nc, *args)
    r = run_bass_kernel_spmd(nc, [arrays], core_ids=[0])
    out = r.results[0]["outT"]
    return out.transpose(1, 0, 2).reshape(D, SEQ).T.reshape(1, SEQ, D)
```

```python
import concourse.bass as bass
from concourse import mybir
from contextlib import ExitStack

F32 = mybir.dt.float32
F32R = mybir.dt.float32r
ALU = mybir.AluOpType
ACT = mybir.ActivationFunctionType
ds = bass.ds

P = 128
D = 1024
SEQ = 1024
DT = D // P
HALF = 512
FF = 2816
FT = FF // P
CHUNKS = FT // 2
HEADS, DH = 8, 64
PAIRS = HEADS // 2
TAPS = 31
CHAIN = TAPS + 1
EPS = 1e-6
NEG = -1e30
SLOTS = 6
UNIT = 1024

U_FFN1 = 0
U_PROJ = U_FFN1 + 6 * CHUNKS
U_V = U_PROJ + 4 * PAIRS
U_WO = U_V + 4
U_FFN2 = U_WO + DT
UNITS = U_FFN2 + 6 * CHUNKS + 4

FILL = {"ffn1": 0, "proj": CHUNKS, "v": CHUNKS + 4, "wo": CHUNKS + 5, "ffn2": CHUNKS + 7}
FILL45 = {"ffn1": 0, "ffn2": CHUNKS}
BANKUSE = {"ffn1": 0, "proj": 2 * CHUNKS, "ffn2": 2 * CHUNKS + 2 * PAIRS}
DUSE = {"ffn1": 0, "ffn2": 16 * CHUNKS}
AHEAD = {"ffn1": 4, "proj": 2, "ffn2": 2}

C_G = {"ffn1": 0, "proj": 8, "ffn2": 16}
C_CW = 24
C_CB = C_CW + 4 * TAPS
C_LG = C_CB + 4
C_LB = C_LG + 4
C_QG = C_LB + 4
C_KG = C_QG + 1
C_N = C_KG + 1


def build(nc, xT, stream, smalls, cols_in, ident_in, table_in, outT):
    h_spill = nc.dram_tensor("h_spill", (P, DT * SEQ), F32).ap()
    ctx = ExitStack()
    with ctx:
        def sb(name, shape, dt):
            return ctx.enter_context(nc.sbuf_tensor(name, shape, dt))

        def sem(name):
            return ctx.enter_context(nc.semaphore(name))

        xh = sb("xh", [P, 8, SEQ], F32R)
        xl = sb("xl", [P, 8, SEQ], F32R)
        h = sb("h", [P, 8, SEQ], F32)
        wraw = sb("wraw", [P, 2, UNIT], F32)
        wh = sb("wh", [P, SLOTS, UNIT], F32R)
        wl = sb("wl", [P, SLOTS, UNIT], F32R)
        ah = sb("ah", [P, 2, SEQ], F32R)
        al = sb("al", [P, 2, SEQ], F32R)
        y = sb("y", [P, 4, SEQ], F32)
        glu = sb("glu", [P, TAPS - 1 + SEQ], F32)
        tmp = sb("tmp", [P, 4, HALF], F32)
        rt = sb("rt", [P, 4, HALF], F32)
        sm = sb("sm", [P, 160], F32)
        consts = sb("consts", [P, C_N], F32)
        eps_col = sb("eps_col", [P, 2], F32)
        negqg = sb("negqg", [P, 1], F32)
        cols = sb("cols", [P, 4], F32)
        ident = sb("ident", [P, P], F32)
        negmax = sb("negmax", [P, 32], F32)
        rowsum = sb("rowsum", [P, 32], F32)
        rowinv = sb("rowinv", [P, 32], F32)
        ps = ctx.enter_context(nc.psum_tensor("ps", [P, 8, 512], F32))

        def flat(buf, first, n):
            return buf[:, first:, :].rearrange("p a n -> p (a n)")[:, 0:n]

        def th(t):
            return slice(t * HALF, (t + 1) * HALF)

        scores = [wraw[:, 0, :], wraw[:, 1, :], flat(tmp, 0, 1024), flat(rt, 0, 1024)]
        table = flat(rt, 2, 1024)
        v_hi = [flat(ah, 0, 2048), flat(al, 0, 2048)]
        v_lo = [flat(wh, 4, 2048), flat(wl, 4, 2048)]
        V_HI = [wh[:, 0, :], wh[:, 2, :]]
        V_LO = [wh[:, 1, :], wh[:, 3, :]]
        def probs(n):
            b, k = n // 16, (n // 2) % 2
            room = flat(wl, 2 + k, 1024) if n % 2 else flat(xl, 4 * b + 1, 2048) if k else flat(wl, 0, 2048)
            return room.rearrange("p (j a q) -> p j a q", a=2, q=P)

        eps_ready = sem("eps_ready")
        x_in = [[sem(f"x_in{t}_{d}") for d in range(4)] for t in range(2)]
        c_in = sem("c_in")
        raw_in = [sem(f"raw_in{r}") for r in range(2)]
        w_hi = [sem(f"w_hi{s}") for s in range(SLOTS)]
        w_lo = [sem(f"w_lo{s}") for s in range(SLOTS)]
        done = [[sem(f"done{s}_{t}") for t in range(2)] for s in range(4)]
        down_last = sem("down_last")
        gbank = [sem(f"gbank{t}") for t in range(2)]
        ubank = [sem(f"ubank{t}") for t in range(2)]
        a_hi = [sem(f"a_hi{t}") for t in range(2)]
        a_lo = [sem(f"a_lo{t}") for t in range(2)]
        down = sem("down")
        dbank = sem("dbank")
        norms = {}
        for ph in ("ffn1", "proj", "ffn2"):
            norms[ph] = {k: sem(f"{ph}_{k}") for k in ("sq", "acc", "stat", "root", "inv", "spread", "scale", "xn", "hi", "lo0", "lo1")}
        spilled = sem("spilled")
        glu_zero = sem("glu_zero")
        tapc = sem("tapc")
        qk_sq = sem("qk_sq")
        qk_stat = sem("qk_stat")
        qk_rooted = sem("qk_rooted")
        qk_inv = sem("qk_inv")
        qk_spread = sem("qk_spread")
        qk_scale = sem("qk_scale")
        qk_n = sem("qk_n")
        qg_neg = sem("qg_neg")
        v_ready = sem("v_ready")
        v_h = sem("v_h")
        v_l = sem("v_l")
        ln = {k: sem(f"ln_{k}") for k in ("mean", "copied", "spread", "m", "cent", "sq", "var", "root", "inv", "vspread",
                                          "v", "scaled", "out")}
        tab_in = sem("tab_in")
        vs_in = [sem(f"vs_in{b}") for b in range(2)]
        st_hi = sem("st_hi")
        st_lo = sem("st_lo")
        st_in = [sem(f"st_in{b}") for b in range(2)]
        carried = sem("carried")
        s_rdy = sem("s_rdy")
        x_rdy = sem("x_rdy")
        p_rdy = sem("p_rdy")
        inv_rdy = sem("inv_rdy")
        pn_rdy = sem("pn_rdy")
        t_rdy = sem("t_rdy")
        pth_rdy = sem("pth_rdy")
        ptl_rdy = sem("ptl_rdy")
        pv_rdy = sem("pv_rdy")
        oh_rdy = sem("oh_rdy")
        o_rdy = sem("o_rdy")
        mix_hi = sem("mix_hi")
        mix_lo = sem("mix_lo")
        h_back = sem("h_back")
        wobank = sem("wobank")
        stored = sem("stored")

        def constants_there(eng):
            eng.wait_ge(c_in, 48)

        block = ctx.enter_context(nc.Block())
        NU = 32
        LAG = 3

        CREDIT = 17

        def unit(n):
            g, r = (n % 16) // 4, n % 4
            return n // 16, 7 - g if r % 2 == 0 else g, 1 - r // 2

        def raw_scores(n):
            return flat(ps, 2 * (n % 2), (unit(n)[1] + 1) * P)

        def turned(n):
            return flat(ps, 3 + 2 * (n % 2), (unit(n)[1] + 1) * P).rearrange("p (j q) -> p j q", q=P)

        def block_of(m):
            return 4 * (m // 2) + 2 + m % 2

        @block.sync
        def _(sp):
            def load_unit(n, r):
                src = stream[ds(n, 1), :, :].rearrange("a p n -> p (a n)")
                sp.dma_start(wraw[:, r, :], src).then_inc(raw_in[r], 16)

            sp.dma_start(cols[:, :], cols_in).then_inc(c_in, 16)
            sp.dma_start(consts[:, :], smalls).then_inc(c_in, 16)
            sp.dma_start(ident[:, :], ident_in).then_inc(c_in, 16)
            for t in range(2):
                for d in range(0, DT, 2):
                    sp.dma_start(h[:, d:d + 2, th(t)], xT[:, d:d + 2, th(t)]).then_inc(x_in[t][d // 2], 16)
                if t == 0:
                    for s in range(2):
                        load_unit(s, s)
            for s in range(2, 4):
                sp.wait_ge(w_lo[s - 2], 1)
                load_unit(s, s % 2)

            def ffn_loads(ph, first):
                f0, f45 = FILL[ph], FILL45[ph]
                with sp.Fori(0, CHUNKS) as i:
                    for s in (4, 5):
                        sp.wait_ge(w_lo[s - 2], i + (f0 + 1))
                        load_unit(i * 6 + (first + s), s % 2)
                    for s in range(4):
                        if s < 2:
                            sp.wait_ge(w_lo[s + 4], i + (f45 + 1))
                        else:
                            sp.wait_ge(w_lo[s - 2], i + (f0 + 2))
                        load_unit(i * 6 + (first + 6 + s), s % 2)

            def four_loads(ph, steps, first):
                f0 = FILL[ph]
                with sp.Fori(0, steps) as i:
                    for s in range(4):
                        sp.wait_ge(w_lo[(s + 2) % 4], i + (f0 + (1 if s < 2 else 2)))
                        load_unit(i * 4 + (first + 4 + s), s % 2)

            ffn_loads("ffn1", U_FFN1)
            for t in range(2):
                sp.wait_ge(dbank, 4 + 16 * (CHUNKS - 1) + 8 * (t + 1))
                sp.dma_start(h_spill.rearrange("p (d n) -> p d n", d=DT)[:, :, th(t)], h[:, :, th(t)]).then_inc(spilled, 16)
            four_loads("proj", PAIRS, U_PROJ)
            sp.wait_ge(ln["v"], 2)
            sp.dma_start(table, table_in).then_inc(tab_in, 16)

            sp.wait_ge(v_l, 8)
            with sp.Fori(0, 2) as it:
                for b in range(2):
                    sp.wait_ge(pv_rdy, it * NU + (16 * b + 1))
                    for dst, src in ((V_HI[b], v_hi), (V_LO[b], v_lo)):
                        for q in range(2):
                            sp.dma_start(
                                dst.bitcast(F32).rearrange("p (t c) -> p t c", c=P)[:, 4 * q:4 * q + 4, :],
                                src[q].bitcast(F32).rearrange("p (t c) -> p t c", c=HALF)[:, :, ds(it * (2 * P) + b * P, P)],
                            ).then_inc(vs_in[b], 16)
                    sp.wait_ge(st_lo, it * 4 + (2 * b + 2))
                    k0 = 4 * b
                    qh, ql, kh = xl[:, k0, :], xl[:, k0 + 1, :], xl[:, k0 + 2, :]
                    lo, hi = slice(0, DH), slice(DH, P)
                    for dst, src in (
                        (xh[hi, k0 + 1, :], qh[hi, :]), (xh[lo, k0 + 1, :], ql[hi, :]),
                        (xh[lo, k0 + 3, :], kh[hi, :]), (xh[hi, k0 + 3, :], kh[hi, :]),
                        (xh[lo, k0, :], qh[lo, :]), (xh[hi, k0, :], ql[lo, :]),
                        (xh[lo, k0 + 2, :], kh[lo, :]), (xh[hi, k0 + 2, :], kh[lo, :]),
                    ):
                        sp.dma_start(dst.bitcast(F32), src.bitcast(F32)).then_inc(st_in[b], 16)
            for d in range(DT):
                sp.wait_ge(mix_lo, 8)
                sp.dma_start(h[:, d, :], h_spill[:, d * SEQ:(d + 1) * SEQ]).then_inc(h_back, 16)
            four_loads("wo", 2, U_WO)
            ffn_loads("ffn2", U_FFN2)
            for q in range(16):
                t, d = q // 8, q % 8
                sp.wait_ge(dbank, 4 + DUSE["ffn2"] + 16 * (CHUNKS - 1) + q + 1)
                sp.dma_start(outT[:, d, th(t)], h[:, d, th(t)]).then_inc(stored, 16)
            sp.wait_ge(stored, 256)

        @block.gpsimd
        def _(pool):
            pool.memset(glu[:, 0:TAPS - 1], 0.0).then_inc(glu_zero, 1)

            def norm_sums(ph):
                m = norms[ph]
                for t in range(2):
                    acc = rt[:, 2 + t, :]
                    for d in range(1, DT):
                        pool.wait_ge(m["sq"], 8 * t + d + 1)
                        if d == 1:
                            pool.tensor_tensor(acc, tmp[:, 0, :], tmp[:, 1, :], ALU.add).then_inc(m["acc"], 1)
                        else:
                            pool.wait_ge(m["acc"], 7 * t + d - 1)
                            pool.tensor_tensor(acc, acc, tmp[:, d % 2, :], ALU.add).then_inc(m["acc"], 1)

            norm_sums("ffn1")
            norm_sums("proj")
            with pool.Fori(0, PAIRS) as i:
                for s in range(4):
                    pool.wait_ge(w_hi[s], i + (FILL["proj"] + 2))
                    pool.tensor_tensor(wl[:, s, :], wraw[:, s % 2, :], wh[:, s, :].bitcast(F32), ALU.subtract).then_inc(w_lo[s], 1)

            pool.wait_ge(qk_n, 4 * PAIRS)
            pool.wait_ge(done[3][1], FILL["v"] + 1)
            with pool.Fori(0, 2) as it:
                for b in range(2):
                    pool.wait_ge(pv_rdy, it * NU + (16 * b + 1))
                    q_k = [h[:, ds(it * 4 + (2 * b + which), 1), :].rearrange("p a n -> p (a n)") for which in range(2)]
                    for which in range(2):
                        pool.tensor_copy(xl[:, 4 * b + 2 * which, :], q_k[which]).then_inc(st_hi, 1)
                    pool.wait_ge(st_hi, it * 4 + (2 * b + 2))
                    pool.sem_inc(carried, 1)
                    for which in range(2):
                        pool.tensor_tensor(xl[:, 4 * b + 2 * which + 1, :], q_k[which], xl[:, 4 * b + 2 * which, :].bitcast(F32),
                                           ALU.subtract).then_inc(st_lo, 1)
            norm_sums("ffn2")

        @block.scalar
        def _(act):
            def norm_squares(ph):
                m = norms[ph]
                for t in range(2):
                    for d in range(DT):
                        if ph == "ffn1":
                            act.wait_ge(x_in[t][d // 2], 16)
                        elif ph == "proj":
                            act.wait_ge(dbank, 4 + 16 * (CHUNKS - 1) + 8 * t + d + 1)
                        else:
                            act.wait_ge(wobank, 4 + 2 * d + t + 1)
                        q = 8 * t + d
                        if q >= 2:
                            act.wait_ge(m["acc"], 7 * t + d - 2 if d > 2 else (7 * t + 1 if d == 2 else 7 * t))
                        nc.scalar.activation(tmp[:, d % 2, :], h[:, d, th(t)], ACT.Square).then_inc(m["sq"], 1)

            def norm_rest(ph):
                m = norms[ph]
                def spread(t):
                    act.wait_ge(m["inv"], t + 1)
                    nc.scalar.activation(rt[:, t, :].rearrange("p (b c) -> p b c", c=P),
                                         sm[:, 4 * t:4 * t + 4].unsqueeze(2).to_broadcast([P, 4, P]), ACT.Copy).then_inc(m["spread"], 1)

                def root(t):
                    act.wait_ge(m["stat"], t + 1)
                    nc.scalar.activation(sm[:, 4 * t:4 * t + 4], ps[:, 2, 4 * t:4 * t + 4], ACT.Sqrt, bias=eps_col[:, 0:1]).then_inc(m["root"], 1)

                root(0)
                spread(0)
                for t in range(2):
                    for d in range(DT):
                        if t == 0 and d == AHEAD[ph]:
                            root(1)
                            spread(1)
                        act.wait_ge(m["xn"], 8 * t + d + 1)
                        nc.scalar.activation(xh[:, d, th(t)], tmp[:, 2 + d % 2, :], ACT.Copy).then_inc(m["hi"], 1)

            def ffn(ph):
                f0, f45, b0 = FILL[ph], FILL45[ph], BANKUSE[ph]
                u0 = {"ffn1": U_FFN1, "ffn2": U_FFN2}[ph]
                with act.Fori(0, CHUNKS) as i:
                    for f in range(2):
                        for t in range(2):
                            n = 2 * f + t
                            act.wait_ge(done[2 * f][t], i + (f0 + 1))
                            act.wait_ge(ubank[t], i * 2 + (b0 + f + 1))
                            nc.scalar.activation(tmp[:, t, :], ps[:, 2 * t, :], ACT.Silu).then_inc(gbank[t], 1)
                            if n == 0:
                                for s in (4, 5):
                                    act.wait_ge(down_last, i + (f45 + 1))
                                    act.wait_ge(raw_in[s % 2], i * 48 + 16 * ((u0 + s) // 2 + 1))
                                    nc.scalar.activation(wh[:, s, :], wraw[:, s % 2, :], ACT.Copy).then_inc(w_hi[s], 1)
                            act.wait_ge(ubank[t], i * 2 + (b0 + f + 2))
                            nc.scalar.activation(ah[:, f, th(t)], tmp[:, 2 + t, :], ACT.Copy).then_inc(a_hi[t], 1)
                            if t == 1:
                                for s in (2 * f, 2 * f + 1):
                                    act.wait_ge(done[s][1], i + (f0 + 1))
                                    act.wait_ge(raw_in[s % 2], i * 48 + 16 * ((u0 + 6 + s) // 2 + 1))
                                    nc.scalar.activation(wh[:, s, :], wraw[:, s % 2, :], ACT.Copy).then_inc(w_hi[s], 1)

            act.sem_inc(down_last, 1)
            for t in range(2):
                act.sem_inc(ubank[t], 1)
            act.wait_ge(eps_ready, 2)
            norm_squares("ffn1")
            for s in range(4):
                act.wait_ge(raw_in[s % 2], 16 * (s // 2 + 1))
                nc.scalar.activation(wh[:, s, :], wraw[:, s % 2, :], ACT.Copy).then_inc(w_hi[s], 1)
            norm_rest("ffn1")
            ffn("ffn1")
            norm_squares("proj")
            norm_rest("proj")

            f0, b0 = FILL["proj"], BANKUSE["proj"]
            act.wait_ge(spilled, 32)
            with act.Fori(0, PAIRS) as i:
                for t in range(2):
                    act.wait_ge(done[0][t], i + (f0 + 1))
                    act.wait_ge(ubank[t], i * 2 + (b0 + 1))
                    nc.scalar.activation(tmp[:, t, :], ps[:, 2 * t, :], ACT.Sigmoid).then_inc(gbank[t], 1)
                for s in (0, 1):
                    act.wait_ge(done[s][1], i + (f0 + 1))
                    act.wait_ge(raw_in[s % 2], i * 32 + 16 * ((U_PROJ + 4 + s) // 2 + 1))
                    nc.scalar.activation(wh[:, s, :], wraw[:, s % 2, :], ACT.Copy).then_inc(w_hi[s], 1)
                for t in range(2):
                    constants_there(act)
                    act.wait_ge(done[2][t], i + (f0 + 1))
                    nc.scalar.activation(h[:, ds(i * 2, 1), th(t)].rearrange("p a n -> p (a n)"), ps[:, 2 * t, :], ACT.Copy).then_inc(gbank[t], 1)
                    constants_there(act)
                    act.wait_ge(done[3][t], i + (f0 + 1))
                    nc.scalar.activation(h[:, ds(i * 2 + 1, 1), th(t)].rearrange("p a n -> p (a n)"), ps[:, 2 * t + 1, :], ACT.Copy).then_inc(ubank[t], 1)
                for s in (2, 3):
                    act.wait_ge(done[s][1], i + (f0 + 1))
                    act.wait_ge(raw_in[s % 2], i * 32 + 16 * ((U_PROJ + 4 + s) // 2 + 1))
                    nc.scalar.activation(wh[:, s, :], wraw[:, s % 2, :], ACT.Copy).then_inc(w_hi[s], 1)

            def v_out(tt):
                if tt in (3, 7):
                    act.wait_ge(done[3][tt // 4], FILL["v"] + 1)
                else:
                    act.wait_ge(v_ready, tt + 1 - (tt > 3))
                nc.scalar.activation(v_hi[tt // 4][:, (tt % 4) * 512:(tt % 4 + 1) * 512], ps[:, 4 + tt % 2, :], ACT.Copy).then_inc(v_h, 1)

            def qk_squares(j):
                for t in range(2):
                    act.wait_ge(ubank[t], b0 + 2 * PAIRS + 1)
                if j >= 1:
                    act.wait_ge(qk_stat, j)
                for which in range(2):
                    nc.scalar.activation(flat(tmp, 2 * which, 1024), h[:, 2 * j + which, :], ACT.Square).then_inc(qk_sq, 1)

            def qk_root(j):
                act.wait_ge(qk_stat, j + 1)
                nc.scalar.activation(sm[:, 32 * j:32 * j + 32], ps[:, 6, 32 * j:32 * j + 32], ACT.Sqrt, bias=eps_col[:, 0:1]).then_inc(qk_rooted, 1)

            def qk_spreads(j):
                act.wait_ge(qk_inv, j + 1)
                if j == 0:
                    act.wait_ge(tapc, PAIRS * CHAIN + 1)
                if j >= 1:
                    act.wait_ge(qk_scale, j)
                nc.scalar.activation(flat(rt, 0, 2048).rearrange("p (b c) -> p b c", c=DH),
                                     sm[:, 32 * j:32 * j + 32].unsqueeze(2).to_broadcast([P, 32, DH]), ACT.Copy).then_inc(qk_spread, 1)

            def ln_spread(cols_at, ready, out):
                act.wait_ge(ready, 1)
                nc.scalar.activation(flat(rt, 0, 1024).rearrange("p (b c) -> p b c", c=P),
                                     sm[:, cols_at:cols_at + 8].unsqueeze(2).to_broadcast([P, 8, P]), ACT.Copy).then_inc(out, 1)

            qk_squares(0)
            v_out(0)
            v_out(1)
            v_out(2)
            for j in range(PAIRS):
                qk_root(j)
                qk_spreads(j)
                v_out(3 + j)
                if j + 1 < PAIRS:
                    qk_squares(j + 1)
            v_out(7)

            act.wait_ge(ln["mean"], 1)
            nc.scalar.activation(sm[:, 128:136], ps[:, 6, 128:136], ACT.Copy).then_inc(ln["copied"], 1)
            ln_spread(128, ln["copied"], ln["spread"])
            for k in range(4):
                act.wait_ge(ln["cent"], 8 if k == 3 else k + 5)
                dst = flat(tmp, 2 * (k % 2), 1024) if k < 2 else flat(rt, 2 * (k % 2), 1024)
                if k == 2:
                    act.wait_ge(ln["m"], 2)
                nc.scalar.activation(dst, y[:, k, :], ACT.Square).then_inc(ln["sq"], 1)
            act.wait_ge(ln["var"], 1)
            nc.scalar.activation(sm[:, 136:144], ps[:, 6, 136:144], ACT.Sqrt, bias=eps_col[:, 0:1]).then_inc(ln["root"], 1)
            ln_spread(136, ln["inv"], ln["vspread"])
            for k in range(4):
                act.wait_ge(ln["scaled"], 2 * k + 2)
                nc.scalar.activation(y[:, k, :], y[:, k, :], ACT.Silu, bias=consts[:, C_LB + k:C_LB + k + 1]).then_inc(ln["out"], 1)

            with act.Fori(0, 2) as it:
                def probs_hi(n):
                    b, i, e = unit(n)
                    act.wait_ge(t_rdy, it * NU + (n + 1))
                    if n >= 4:
                        act.wait_ge(pv_rdy, it * NU + (CREDIT + n - 3))
                    nc.scalar.activation(probs(n)[:, 0:i + 1, 0, :], turned(n), ACT.Copy).then_inc(pth_rdy, 1)

                def out_half(m):
                    n = block_of(m)
                    act.wait_ge(pv_rdy, it * NU + (CREDIT + n + 1))
                    for e in range(2):
                        nc.scalar.activation(glu[DH * e:DH * e + DH, (m % 2) * P:(m % 2 + 1) * P],
                                             ps[DH * e:DH * e + DH, 6 + m % 2, 2 * P * e:2 * P * e + P], ACT.Copy).then_inc(oh_rdy, 1)

                for n in range(NU + LAG + 2):
                    if LAG <= n < NU + LAG:
                        probs_hi(n - LAG)
                    if n < NU:
                        b, i, e = unit(n)
                        nk = (i + 1) * P
                        act.wait_ge(x_rdy, it * NU + (n + 1))
                        nc.scalar.activation(scores[n % 4][:, 0:nk], scores[n % 4][:, 0:nk], ACT.Exp, bias=negmax[:, n:n + 1],
                                             scale=-1.0, accum_out=rowsum[:, n:n + 1]).then_inc(p_rdy, 1)
                    k = n - LAG - 2
                    if k >= 0 and k % 4 >= 2:
                        out_half(2 * (k // 4) + k % 2)

            act.wait_ge(ptl_rdy, 2 * NU)
            act.wait_ge(pv_rdy, 2 * NU + CREDIT)
            for s in range(2):
                act.dma_start(wraw[:, s, :], stream[U_WO + s, :, :]).then_inc(raw_in[s], 16)

            def wo_unit(s):
                act.wait_ge(raw_in[s % 2], 16 * ((U_WO + s) // 2 + 1))
                nc.scalar.activation(wh[:, s, :], wraw[:, s % 2, :], ACT.Copy).then_inc(w_hi[s], 1)

            def mix(m):
                act.wait_ge(o_rdy, 64)
                src = h[:, 2 * m, :] if m < 4 else y[:, m - 4, :]
                nc.scalar.activation(xh[:, m, :], src, ACT.Copy).then_inc(mix_hi, 1)

            for m in range(DT):
                if m == 2:
                    wo_unit(0)
                    wo_unit(1)
                mix(m)
            for s in (2, 3):
                act.wait_ge(w_lo[s - 2], FILL["wo"] + 1)
                act.dma_start(wraw[:, s % 2, :], stream[U_WO + s, :, :]).then_inc(raw_in[s % 2], 16)
                wo_unit(s)
            f0 = FILL["wo"]
            with act.Fori(0, 2) as i:
                for s in range(4):
                    act.wait_ge(done[s][1], i + (f0 + 1))
                    act.wait_ge(raw_in[s % 2], i * 32 + 16 * ((U_WO + 4 + s) // 2 + 1))
                    nc.scalar.activation(wh[:, s, :], wraw[:, s % 2, :], ACT.Copy).then_inc(w_hi[s], 1)
            norm_squares("ffn2")
            norm_rest("ffn2")
            ffn("ffn2")

        @block.vector
        def _(dve):
            def lo_part(s, value):
                dve.wait_ge(w_hi[s], value)
                nc.vector.tensor_tensor(wl[:, s, :], wraw[:, s % 2, :], wh[:, s, :].bitcast(F32), ALU.subtract).then_inc(w_lo[s], 1)

            def norm(ph):
                m = norms[ph]
                def inverse(t):
                    dve.wait_ge(m["root"], t + 1)
                    nc.vector.reciprocal(sm[:, 4 * t:4 * t + 4], sm[:, 4 * t:4 * t + 4]).then_inc(m["inv"], 1)

                inverse(0)
                for t in range(2):
                    for d in range(DT):
                        q = 8 * t + d
                        if q == AHEAD[ph]:
                            inverse(1)
                        dve.wait_ge(m["scale"], t + 1)
                        g = C_G[ph] + d
                        nc.vector.scalar_tensor_tensor(out=tmp[:, 2 + d % 2, :], in0=h[:, d, th(t)], scalar=consts[:, g:g + 1],
                                                       in1=ps[:, 3 + 4 * t, :], op0=ALU.mult, op1=ALU.mult).then_inc(m["xn"], 1)
                        dve.wait_ge(m["hi"], q + 1)
                        nc.vector.tensor_tensor(xl[:, d, th(t)], tmp[:, 2 + d % 2, :], xh[:, d, th(t)].bitcast(F32),
                                                ALU.subtract).then_inc(m[f"lo{t}"], 1)

            def ffn(ph):
                f0, f45, b0, d0 = FILL[ph], FILL45[ph], BANKUSE[ph], DUSE[ph]
                with dve.Fori(0, CHUNKS) as i:
                    def gated(f, t):
                        dve.wait_ge(gbank[t], i * 2 + (b0 + f + 2))
                        dve.wait_ge(done[2 * f + 1][t], i + (f0 + 1))
                        nc.vector.tensor_tensor(tmp[:, 2 + t, :], tmp[:, t, :], ps[:, 2 * t + 1, :], ALU.mult).then_inc(ubank[t], 1)
                        dve.wait_ge(a_hi[t], i * 2 + (b_ffn + f + 1))
                        nc.vector.tensor_tensor(al[:, f, th(t)], tmp[:, 2 + t, :], ah[:, f, th(t)].bitcast(F32),
                                                ALU.subtract).then_inc(a_lo[t], 1)

                    def add_down(q):
                        t, d = q // 8, q % 8
                        if q == 15:
                            dve.wait_ge(down_last, i + (f45 + 2))
                        else:
                            dve.wait_ge(down, i * 15 + (15 * d0 // 16 + q + 1))
                        nc.vector.scalar_tensor_tensor(out=h[:, d, th(t)], in0=ps[:, 4 + q % 4, :], scalar=0.5,
                                                       in1=h[:, d, th(t)], op0=ALU.mult, op1=ALU.add).then_inc(dbank, 1)

                    b_ffn = {"ffn1": 0, "ffn2": 2 * CHUNKS}[ph]
                    gated(0, 0)
                    lo_part(4, i + (f45 + 1))
                    lo_part(5, i + (f45 + 1))
                    gated(0, 1)
                    lo_part(0, i + (f0 + 2))
                    lo_part(1, i + (f0 + 2))
                    gated(1, 0)
                    gated(1, 1)
                    for q in range(16):
                        add_down(q)
                        if q == 3:
                            lo_part(2, i + (f0 + 2))
                            lo_part(3, i + (f0 + 2))

            dve.sem_inc(tapc, 1)
            nc.vector.memset(eps_col[:, 0:1], EPS).then_inc(eps_ready, 1)
            nc.vector.memset(eps_col[:, 1:2], 64 * EPS).then_inc(eps_ready, 1)
            dve.wait_ge(c_in, 48)
            nc.vector.tensor_scalar(negqg[:, :], consts[:, C_QG:C_QG + 1], -0.125, None, ALU.mult).then_inc(qg_neg, 1)
            for s in range(4):
                lo_part(s, 1)
            norm("ffn1")
            ffn("ffn1")
            norm("proj")

            f0, b0 = FILL["proj"], BANKUSE["proj"]
            dve.wait_ge(qg_neg, 1)
            dve.wait_ge(glu_zero, 1)
            with dve.Fori(0, PAIRS) as i:
                dve.wait_ge(tapc, i * CHAIN + 1)
                for t in range(2):
                    dve.wait_ge(gbank[t], i * 2 + (b0 + 2))
                    dve.wait_ge(done[1][t], i + (f0 + 1))
                    nc.vector.tensor_tensor(glu[:, TAPS - 1 + t * HALF:TAPS - 1 + (t + 1) * HALF], tmp[:, t, :], ps[:, 2 * t + 1, :],
                                            ALU.mult).then_inc(ubank[t], 1)
                ytile = y[:, ds(i, 1), :].rearrange("p a n -> p (a n)")
                odd = flat(rt, 0, SEQ)
                for k in range(TAPS):
                    if k == 0:
                        dve.wait_ge(ubank[1], i * 2 + (b0 + 2))
                        nc.vector.tensor_scalar(ytile, glu[:, 0:SEQ], consts[:, ds(i * TAPS + C_CW, 1)], consts[:, ds(i + C_CB, 1)],
                                                ALU.mult, ALU.add).then_inc(tapc, 1)
                    elif k == 1:
                        nc.vector.tensor_scalar(odd, glu[:, 1:1 + SEQ], consts[:, ds(i * TAPS + (C_CW + 1), 1)], None,
                                                ALU.mult).then_inc(tapc, 1)
                    else:
                        total = odd if k % 2 else ytile
                        dve.wait_ge(tapc, i * CHAIN + k)
                        nc.vector.scalar_tensor_tensor(out=total, in0=glu[:, k:k + SEQ], scalar=consts[:, ds(i * TAPS + (C_CW + k), 1)],
                                                       in1=total, op0=ALU.mult, op1=ALU.add).then_inc(tapc, 1)
                dve.wait_ge(tapc, i * CHAIN + (TAPS + 1))
                nc.vector.tensor_tensor(ytile, ytile, odd, ALU.add).then_inc(tapc, 1)

            def v_out(tt):
                dve.wait_ge(v_h, tt + 1)
                c = slice((tt % 4) * 512, (tt % 4 + 1) * 512)
                nc.vector.tensor_tensor(v_lo[tt // 4][:, c], ps[:, 4 + tt % 2, :], v_hi[tt // 4][:, c].bitcast(F32),
                                        ALU.subtract).then_inc(v_l, 1)

            def qk_inverse(j):
                dve.wait_ge(qk_rooted, j + 1)
                nc.vector.reciprocal(sm[:, 32 * j:32 * j + 32], sm[:, 32 * j:32 * j + 32]).then_inc(qk_inv, 1)

            def qk_scaled(j):
                dve.wait_ge(qk_scale, j + 1)
                for n in range(4):
                    tile = h[:, 2 * j + n // 2, th(n % 2)]
                    gain = consts[:, C_KG:C_KG + 1] if n >= 2 else negqg[:, 0:1]
                    nc.vector.scalar_tensor_tensor(out=tile, in0=tile, scalar=gain, in1=ps[:, n, :], op0=ALU.mult,
                                                   op1=ALU.mult).then_inc(qk_n, 1)

            v_out(0)
            v_out(1)
            v_out(2)
            for j in range(PAIRS):
                qk_inverse(j)
                v_out(3 + j)
                qk_scaled(j)
            v_out(7)

            dve.wait_ge(ln["m"], 2)
            for k in range(4):
                for t in range(2):
                    nc.vector.tensor_tensor(y[:, k, th(t)], y[:, k, th(t)], ps[:, t, :], ALU.subtract).then_inc(ln["cent"], 1)
            dve.wait_ge(ln["root"], 1)
            nc.vector.reciprocal(sm[:, 136:144], sm[:, 136:144]).then_inc(ln["inv"], 1)
            dve.wait_ge(ln["v"], 2)
            dve.wait_ge(ln["sq"], 4)
            for k in range(4):
                for t in range(2):
                    nc.vector.scalar_tensor_tensor(out=y[:, k, th(t)], in0=y[:, k, th(t)], scalar=consts[:, C_LG + k:C_LG + k + 1],
                                                   in1=ps[:, 2 + t, :], op0=ALU.mult, op1=ALU.mult).then_inc(ln["scaled"], 1)

            dve.wait_ge(tab_in, 16)
            with dve.Fori(0, 2) as it:
                def masked(n):
                    b, i, e = unit(n)
                    nk = (i + 1) * P
                    if n < 2:
                        dve.wait_ge(s_rdy, it * NU + (CREDIT + n + 1))
                        nc.vector.memset(rowinv[:, n:n + 1], 0.0).then_inc(carried, 1)
                    nc.vector.tensor_tensor_reduce(scores[n % 4][:, 0:nk], raw_scores(n), table[:, SEQ - nk:SEQ], 1.0, 3e38,
                                                   ALU.add, ALU.min, negmax[:, n:n + 1]).then_inc(x_rdy, 1)

                def normalised(n):
                    b, i, e = unit(n)
                    nk = (i + 1) * P
                    dve.wait_ge(p_rdy, it * NU + (n + 1))
                    nc.vector.reciprocal(rowinv[:, n:n + 1], rowsum[:, n:n + 1]).then_inc(inv_rdy, 1)
                    dve.wait_ge(inv_rdy, it * NU + (n + 1))
                    if n + 2 < NU:
                        dve.wait_ge(s_rdy, it * NU + (CREDIT + n + 3))
                    nc.vector.tensor_scalar(scores[n % 4][:, 0:nk], scores[n % 4][:, 0:nk], rowinv[:, n:n + 1], None,
                                            ALU.mult).then_inc(pn_rdy, 1)

                def probs_lo(n):
                    b, i, e = unit(n)
                    dve.wait_ge(pth_rdy, it * NU + (n + 1))
                    nc.vector.tensor_tensor(probs(n)[:, 0:i + 1, 1, :], turned(n), probs(n)[:, 0:i + 1, 0, :].bitcast(F32),
                                            ALU.subtract).then_inc(ptl_rdy, 1)

                def heads_out(m):
                    b, i, e = unit(block_of(m))
                    for e in range(2):
                        rows = slice(DH * e, DH * e + DH)
                        dve.wait_ge(oh_rdy, it * NU + (2 * m + e + 1))
                        nc.vector.tensor_tensor(h[rows, ds(it * 4 + 2 * b, 1), i * P:(i + 1) * P].rearrange("p a n -> p (a n)"),
                                                ps[rows, 6 + m % 2, 2 * P * e + P:2 * P * e + 2 * P],
                                                glu[rows, (m % 2) * P:(m % 2 + 1) * P], ALU.add).then_inc(o_rdy, 1)

                for n in range(NU + LAG + 2):
                    if n < NU:
                        masked(n)
                    if 1 <= n <= NU:
                        normalised(n - 1)
                    if LAG <= n < NU + LAG:
                        probs_lo(n - LAG)
                    k = n - LAG - 2
                    if k >= 0 and k % 4 >= 2:
                        heads_out(2 * (k // 4) + k % 2)

            def mix(m):
                dve.wait_ge(mix_hi, m + 1)
                src = h[:, 2 * m, :] if m < 4 else y[:, m - 4, :]
                nc.vector.tensor_tensor(xl[:, m, :], src, xh[:, m, :].bitcast(F32), ALU.subtract).then_inc(mix_lo, 1)

            f0 = FILL["wo"]
            for m in range(DT):
                if m == 2:
                    lo_part(0, f0 + 1)
                    lo_part(1, f0 + 1)
                mix(m)
            for s in (2, 3):
                lo_part(s, f0 + 1)
            with dve.Fori(0, 2) as i:
                for s in range(4):
                    for t in range(2):
                        dve.wait_ge(done[s][t], i + (f0 + 1))
                        dve.wait_ge(h_back, 16 * DT)
                        tile = h[:, ds(i * 4 + s, 1), th(t)].rearrange("p a n -> p (a n)")
                        nc.vector.tensor_tensor(tile, ps[:, 4 + (2 * s + t) % 4, :], tile, ALU.add).then_inc(wobank, 1)
                    lo_part(s, i + (f0 + 2))
            norm("ffn2")
            ffn("ffn2")

        @block.tensor
        def _(pe):
            def three(out, lhs_hi, lhs_lo, rhs_hi, rhs_lo, start, stop):
                nc.tensor.matmul(out, lhs_hi, rhs_hi, start=start, stop=False)
                nc.tensor.matmul(out, lhs_hi, rhs_lo, start=False, stop=False)
                return nc.tensor.matmul(out, lhs_lo, rhs_hi, start=False, stop=stop)

            def turn_scales(bank, spread, blocks):
                for b in range(blocks):
                    mm = nc.tensor.transpose(ps[:, bank + b // 4, (b % 4) * P:(b % 4 + 1) * P], spread[:, b * P:(b + 1) * P], ident[:, :])
                return mm

            def norm_stats(ph):
                m = norms[ph]
                for t in range(2):
                    pe.wait_ge(m["acc"], 7 * (t + 1))
                    for b in range(4):
                        mm = nc.tensor.matmul(ps[:, 2, 4 * t + b:4 * t + b + 1], rt[:, 2 + t, b * P:(b + 1) * P], cols[:, 0:1],
                                              start=True, stop=True)
                    mm.then_inc(m["stat"], 1)
                    pe.wait_ge(m["spread"], t + 1)
                    turn_scales(3 + 4 * t, rt[:, t, :], 4).then_inc(m["scale"], 1)

            def column(bank, s, t, ready=None):
                for d in range(DT):
                    if ready is not None:
                        pe.wait_ge(ready, d + 1)
                    c = slice(d * P, (d + 1) * P)
                    mm = three(ps[:, bank, :], wh[:, s, c], wl[:, s, c], xh[:, d, th(t)], xl[:, d, th(t)], d == 0, d == DT - 1)
                return mm

            def ffn(ph):
                f0, f45, b0, d0 = FILL[ph], FILL45[ph], BANKUSE[ph], DUSE[ph]
                b_ffn = {"ffn1": 0, "ffn2": 2 * CHUNKS}[ph]
                with pe.Fori(0, CHUNKS) as i:
                    for f in range(2):
                        for t in range(2):
                            ready = norms[ph][f"lo{t}"] if f == 0 else None
                            pe.wait_ge(gbank[t], i * 2 + (b0 + f + 1))
                            if t == 0:
                                pe.wait_ge(w_lo[2 * f], i + (f0 + 1))
                            column(2 * t, 2 * f, t, ready).then_inc(done[2 * f][t], 1)
                            pe.wait_ge(ubank[t], i * 2 + (b0 + f + 1))
                            if t == 0:
                                pe.wait_ge(w_lo[2 * f + 1], i + (f0 + 1))
                            column(2 * t + 1, 2 * f + 1, t).then_inc(done[2 * f + 1][t], 1)
                    for q in range(16):
                        t, d = q // 8, q % 8
                        if q == 0:
                            pe.wait_ge(w_lo[4], i + (f45 + 1))
                            pe.wait_ge(w_lo[5], i + (f45 + 1))
                        if d == 0:
                            pe.wait_ge(a_lo[t], i * 2 + (b_ffn + 2))
                        pe.wait_ge(dbank, i * 16 + (d0 + q + 1))
                        c = slice(d * P, (d + 1) * P)
                        for f in range(2):
                            mm = three(ps[:, 4 + q % 4, :], wh[:, 4 + f, c], wl[:, 4 + f, c], ah[:, f, th(t)], al[:, f, th(t)], f == 0, f == 1)
                        mm.then_inc(down_last if q == 15 else down, 1)

            for t in range(2):
                pe.sem_inc(gbank[t], 1)
            pe.sem_inc(dbank, 4)
            pe.sem_inc(wobank, 4)
            pe.sem_inc(pv_rdy, CREDIT)
            pe.sem_inc(s_rdy, CREDIT)
            pe.wait_ge(c_in, 48)
            norm_stats("ffn1")
            ffn("ffn1")
            norm_stats("proj")
            f0, b0 = FILL["proj"], BANKUSE["proj"]
            with pe.Fori(0, PAIRS) as i:
                for part in range(2):
                    for t in range(2):
                        ready = norms["proj"][f"lo{t}"] if part == 0 else None
                        pe.wait_ge(gbank[t], i * 2 + (b0 + part + 1))
                        if t == 0:
                            pe.wait_ge(w_lo[2 * part], i + (f0 + 1))
                        column(2 * t, 2 * part, t, ready).then_inc(done[2 * part][t], 1)
                        pe.wait_ge(ubank[t], i * 2 + (b0 + part + 1))
                        if t == 0:
                            pe.wait_ge(w_lo[2 * part + 1], i + (f0 + 1))
                        column(2 * t + 1, 2 * part + 1, t).then_inc(done[2 * part + 1][t], 1)

            def v_rows(tt):
                if tt >= 2:
                    pe.wait_ge(v_l, tt - 1)
                for d in range(DT):
                    s, r = d // 2, d % 2
                    if tt == 0 and r == 0:
                        pe.wait_ge(w_lo[s], FILL["v"] + 1)
                    c = slice(tt * P, (tt + 1) * P)
                    w = slice(r * 512, (r + 1) * 512)
                    mm = three(ps[:, 4 + tt % 2, :], xh[:, d, c], xl[:, d, c], wh[:, s, w], wl[:, s, w], d == 0, d == DT - 1)
                    if tt in (3, 7) and r == 1:
                        mm.then_inc(done[s][tt // 4], 1)
                if tt not in (3, 7):
                    mm.then_inc(v_ready, 1)

            def qk_stats(j):
                pe.wait_ge(qk_sq, 2 * j + 2)
                for n in range(16):
                    mm = nc.tensor.matmul(ps[:, 6, 32 * j + 2 * n:32 * j + 2 * n + 2], flat(tmp, 0, 2048)[:, n * P:(n + 1) * P],
                                          cols[:, 1:3], start=True, stop=True)
                mm.then_inc(qk_stat, 1)

            def qk_turn(j):
                pe.wait_ge(qk_spread, j + 1)
                if j == 0:
                    for t in range(2):
                        pe.wait_ge(gbank[t], b0 + 2 * PAIRS + 1)
                        pe.wait_ge(ubank[t], b0 + 2 * PAIRS + 1)
                else:
                    pe.wait_ge(qk_n, 4 * j)
                turn_scales(0, flat(rt, 0, 2048), 16).then_inc(qk_scale, 1)

            def ln_means(col, src, done_sem):
                for b in range(8):
                    for k in range(4):
                        mm = nc.tensor.matmul(ps[:, 6, col + b:col + b + 1], src(k)[:, b * P:(b + 1) * P], cols[:, 3:4],
                                              start=(k == 0), stop=(k == 3))
                mm.then_inc(done_sem, 1)

            v_rows(0)
            v_rows(1)
            v_rows(2)
            qk_stats(0)
            for j in range(PAIRS):
                v_rows(3 + j)
                qk_turn(j)
                if j + 1 < PAIRS:
                    qk_stats(j + 1)
            pe.wait_ge(tapc, PAIRS * CHAIN + 1)
            ln_means(128, lambda k: y[:, k, :], ln["mean"])
            v_rows(7)
            pe.wait_ge(ln["spread"], 1)
            pe.wait_ge(qk_n, 4 * PAIRS)
            for t in range(2):
                turn_scales(t, rt[:, t, :], 4).then_inc(ln["m"], 1)
            pe.wait_ge(ln["sq"], 4)
            ln_means(136, lambda k: flat(tmp if k < 2 else rt, 2 * (k % 2), 1024), ln["var"])
            pe.wait_ge(ln["vspread"], 1)
            for t in range(2):
                turn_scales(2 + t, rt[:, t, :], 4).then_inc(ln["v"], 1)

            pe.wait_ge(ln["scaled"], 8)
            with pe.Fori(0, 2) as it:
                def score(n):
                    b, i, e = unit(n)
                    if n % 16 == 0:
                        pe.wait_ge(st_in[b], it * 128 + 128)
                    if n >= 2:
                        pe.wait_ge(x_rdy, it * NU + (n - 1))
                    nk = (i + 1) * P
                    rows = slice(DH * e, DH * e + DH)
                    q = slice(i * P, (i + 1) * P)
                    for c in range(0, nk, 512):
                        w = min(512, nk - c)
                        out = ps[:, 2 * (n % 2) + c // 512, 0:w]
                        nc.tensor.matmul(out, xh[:, 4 * b + e, q], xh[:, 4 * b + 2 + e, c:c + w], start=True, stop=False)
                        mm = nc.tensor.matmul(out, xl[rows, 4 * b, q], xl[rows, 4 * b + 3, c:c + w], start=False, stop=True)
                    mm.then_inc(s_rdy, 1)

                def turn(n):
                    b, i, e = unit(n)
                    pe.wait_ge(pn_rdy, it * NU + (n + 1))
                    if n >= 2:
                        pe.wait_ge(ptl_rdy, it * NU + (n - 1))
                    for j in range(i + 1):
                        mm = nc.tensor.transpose(ps[:, 3 + 2 * (n % 2) + j // 4, (j % 4) * P:(j % 4 + 1) * P], scores[n % 4][:, j * P:(j + 1) * P],
                                                 ident[:, :])
                    mm.then_inc(t_rdy, 1)

                def weighted(n):
                    b, i, e = unit(n)
                    m = 2 * (n // 4) + n % 2
                    if n % 16 == 0:
                        pe.wait_ge(vs_in[b], it * 64 + 64)
                    pe.wait_ge(ptl_rdy, it * NU + (n + 1))
                    if e == 1 and m >= 2:
                        pe.wait_ge(o_rdy, it * NU + 2 * (m - 1))
                    out = ps[:, 6 + m % 2, 2 * P * e:2 * P * e + 2 * P]
                    for j in range(i + 1):
                        c = slice(j * P, (j + 1) * P)
                        both = probs(n)[:, j, :, :].rearrange("p a q -> p (a q)")
                        nc.tensor.matmul(out, V_HI[b][:, c], both, start=j == 0, stop=False)
                        mm = nc.tensor.matmul(out, V_LO[b][:, c], both, start=False, stop=j == i)
                    mm.then_inc(pv_rdy, 1)

                score(0)
                score(1)
                for n in range(NU + LAG + 1):
                    if n > LAG:
                        weighted(n - LAG - 1)
                    if n + 2 < NU:
                        score(n + 2)
                    if 1 <= n <= NU:
                        turn(n - 1)

            f0 = FILL["wo"]
            pe.wait_ge(o_rdy, 64)
            with pe.Fori(0, 2) as i:
                for s in range(4):
                    pe.wait_ge(w_lo[s], i + (f0 + 1))
                    for t in range(2):
                        pe.wait_ge(wobank, i * 8 + (2 * s + t + 1))
                        ready = mix_lo if s == 0 and t == 0 else None
                        column(4 + (2 * s + t) % 4, s, t, ready).then_inc(done[s][t], 1)
            norm_stats("ffn2")
            ffn("ffn2")


def kernel(**inputs):
    import numpy as np
    import concourse.bacc as bacc
    from concourse.bass_utils import run_bass_kernel_spmd

    w = {k: np.asarray(v) for k, v in inputs.items()}

    def columns(m):
        return m.reshape(DT, P, -1, P).transpose(2, 1, 0, 3).reshape(-1, P, UNIT)

    def ffn_units(gate, up, down):
        g, u, d = columns(gate), columns(up), down.reshape(FT, P, UNIT)
        return [x for c in range(CHUNKS) for x in (g[2 * c], u[2 * c], g[2 * c + 1], u[2 * c + 1], d[2 * c], d[2 * c + 1])]

    w_in = columns(w["w_in"][0])
    v_units = w["w_in"][0][:, 1024:1536].reshape(4, 2, P, 512).transpose(0, 2, 1, 3).reshape(4, P, UNIT)
    units = ffn_units(w["ffn1_w_gate"][0], w["ffn1_w_up"][0], w["ffn1_w_down"][0])
    for p in range(PAIRS):
        units += [w_in[16 + p], w_in[12 + p], w_in[p], w_in[4 + p]]
    units += list(v_units)
    units += list(columns(w["w_out"][0]))
    units += ffn_units(w["ffn2_w_gate"][0], w["ffn2_w_up"][0], w["ffn2_w_down"][0])
    units += [np.zeros((P, UNIT), np.float32)] * 4

    def tiles(v):
        return v.reshape(-1, P).T

    smalls = np.concatenate([
        tiles(w["ffn1_norm"][0]), tiles(w["mix_norm"][0]), tiles(w["ffn2_norm"][0]),
        w["conv_w"][0].reshape(TAPS, 4, P).transpose(2, 1, 0).reshape(P, 4 * TAPS),
        tiles(w["conv_b"][0]), tiles(w["conv_ln_g"][0]), tiles(w["conv_ln_b"][0]),
        np.tile(w["q_norm"][0], 2)[:, None], np.tile(w["k_norm"][0], 2)[:, None]], axis=1)

    head = np.arange(P) // DH
    cols = np.stack([np.full(P, 1.0 / D), (head == 0) / DH, (head == 1) / DH, np.full(P, 1.0 / 512)], 1).astype(np.float32)
    dist = np.arange(P)[:, None] + (SEQ - P) - np.arange(SEQ)[None, :]
    count = sum(((dist >= 0) & (dist <= window) & (dist % step == 0)).astype(int)
                for window, step in ((128, 1), (512, 4), (2048, 16)))
    table = np.where(count > 0, -np.log(np.maximum(count, 1)), -NEG).astype(np.float32)

    arrays = {
        "xT": w["x"][0].T.reshape(DT, P, SEQ).transpose(1, 0, 2),
        "stream": np.stack(units),
        "smalls": smalls,
        "cols": cols,
        "ident": np.eye(P, dtype=np.float32),
        "table": table,
    }
    arrays = {f"in_{k}": np.ascontiguousarray(v) for k, v in arrays.items()}
    nc = bacc.Bacc("TRN2", target_bir_lowering=False, num_devices=1)
    args = [nc.dram_tensor(k, a.shape, mybir.dt.from_np(a.dtype), kind="ExternalInput").ap() for k, a in arrays.items()]
    args.append(nc.dram_tensor("outT", (P, DT, SEQ), F32, kind="ExternalOutput").ap())
    build(nc, *args)
    r = run_bass_kernel_spmd(nc, [arrays], core_ids=[0])
    out = r.results[0]["outT"]
    return out.transpose(1, 0, 2).reshape(D, SEQ).T.reshape(1, SEQ, D)
```

```python
import concourse.bass as bass
from concourse import mybir
from contextlib import ExitStack

F32 = mybir.dt.float32
F32R = mybir.dt.float32r
ALU = mybir.AluOpType
ACT = mybir.ActivationFunctionType
ds = bass.ds

P = 128
D = 1024
SEQ = 1024
DT = D // P
HALF = 512
FF = 2816
FT = FF // P
CHUNKS = FT // 2
HEADS, DH = 8, 64
PAIRS = HEADS // 2
TAPS = 31
CHAIN = TAPS + 1
EPS = 1e-6
NEG = -1e30
SLOTS = 6
UNIT = 1024

U_FFN1 = 0
U_PROJ = U_FFN1 + 6 * CHUNKS
U_V = U_PROJ + 4 * PAIRS
U_WO = U_V + 4
U_FFN2 = U_WO + 2 * DT
UNITS = U_FFN2 + 6 * CHUNKS + 4

FILL = {"ffn1": 0, "proj": CHUNKS, "v": CHUNKS + 4, "wo": CHUNKS + 5, "ffn2": CHUNKS + 9}
FILL45 = {"ffn1": 0, "ffn2": CHUNKS}
SKIPPED = {"ffn1": (0, 0), "ffn2": (4, 0)}
BANKUSE = {"ffn1": 0, "proj": 2 * CHUNKS, "ffn2": 2 * CHUNKS + 2 * PAIRS}
DUSE = {"ffn1": 0, "ffn2": 16 * CHUNKS}
SUMMED = {"ffn1": (7, 14), "proj": (7, 14), "ffn2": (10, 19)}

C_G = {"ffn1": 0, "proj": 8, "ffn2": 16}
C_CW = 24
C_CB = C_CW + 4 * TAPS
C_LG = C_CB + 4
C_LB = C_LG + 4
C_QG = C_LB + 4
C_KG = C_QG + 1
C_N = C_KG + 1


def build(nc, xT, stream, smalls, cols_in, ident_in, table_in, outT):
    h_spill = nc.dram_tensor("h_spill", (P, DT * SEQ), F32).ap()
    ctx = ExitStack()
    with ctx:
        def sb(name, shape, dt):
            return ctx.enter_context(nc.sbuf_tensor(name, shape, dt))

        def sem(name):
            return ctx.enter_context(nc.semaphore(name))

        xh = sb("xh", [P, 8, SEQ], F32R)
        xl = sb("xl", [P, 8, SEQ], F32R)
        h = sb("h", [P, 8, SEQ], F32)
        wraw = sb("wraw", [P, 2, UNIT], F32)
        wh = sb("wh", [P, SLOTS, UNIT], F32R)
        wl = sb("wl", [P, SLOTS, UNIT], F32R)
        ah = sb("ah", [P, 2, SEQ], F32R)
        al = sb("al", [P, 2, SEQ], F32R)
        y = sb("y", [P, 4, SEQ], F32)
        glu = sb("glu", [P, TAPS - 1 + SEQ], F32)
        tmp = sb("tmp", [P, 4, HALF], F32)
        rt = sb("rt", [P, 4, HALF], F32)
        sm = sb("sm", [P, 160], F32)
        consts = sb("consts", [P, C_N], F32)
        eps_col = sb("eps_col", [P, 3], F32)
        negqg = sb("negqg", [P, 1], F32)
        cols = sb("cols", [P, 4], F32)
        ident = sb("ident", [P, P], F32)
        ones = sb("ones", [P, P], F32)
        negmax = sb("negmax", [P, 32], F32)
        rowsum = sb("rowsum", [P, 32], F32)
        rowinv = sb("rowinv", [P, 32], F32)
        ps = ctx.enter_context(nc.psum_tensor("ps", [P, 8, 512], F32))

        def flat(buf, first, n):
            return buf[:, first:, :].rearrange("p a n -> p (a n)")[:, 0:n]

        def th(t):
            return slice(t * HALF, (t + 1) * HALF)

        scores = [wraw[:, 0, :], wraw[:, 1, :], flat(tmp, 0, 1024), flat(rt, 0, 1024)]
        table = flat(rt, 2, 1024)
        v_hi = [flat(ah, 0, 2048), flat(al, 0, 2048)]
        v_lo = [flat(wh, 4, 2048), flat(wl, 4, 2048)]
        V_HI = [wh[:, 0, :], wh[:, 2, :]]
        V_LO = [wh[:, 1, :], wh[:, 3, :]]
        def probs(n):
            b, k = n // 16, (n // 2) % 2
            room = flat(wl, 2 + k, 1024) if n % 2 else flat(xl, 4 * b + 1, 2048) if k else flat(wl, 0, 2048)
            return room.rearrange("p (j a q) -> p j a q", a=2, q=P)

        eps_ready = sem("eps_ready")
        dummy = sem("dummy")
        x_in = [[sem(f"x_in{t}_{d}") for d in range(4)] for t in range(2)]
        c_in = sem("c_in")
        raw_in = [sem(f"raw_in{r}") for r in range(2)]
        w_hi = [sem(f"w_hi{s}") for s in range(SLOTS)]
        w_lo = [sem(f"w_lo{s}") for s in range(SLOTS)]
        done = [[sem(f"done{s}_{t}") for t in range(2)] for s in range(4)]
        down_last = sem("down_last")
        gbank = [sem(f"gbank{t}") for t in range(2)]
        ubank = [sem(f"ubank{t}") for t in range(2)]
        a_hi = [sem(f"a_hi{t}") for t in range(2)]
        a_lo = [sem(f"a_lo{t}") for t in range(2)]
        down = sem("down")
        dbank = sem("dbank")
        norms = {}
        for ph in ("ffn1", "proj", "ffn2"):
            norms[ph] = {k: sem(f"{ph}_{k}") for k in ("sq", "acc", "stat", "root", "inv", "spread", "scale", "xn", "hi", "lo0", "lo1")}
        spilled = sem("spilled")
        glu_zero = sem("glu_zero")
        tapc = sem("tapc")
        qk_sq = sem("qk_sq")
        qk_stat = sem("qk_stat")
        qk_rooted = sem("qk_rooted")
        qk_inv = sem("qk_inv")
        qk_spread = sem("qk_spread")
        qk_scale = sem("qk_scale")
        qk_n = sem("qk_n")
        qg_neg = sem("qg_neg")
        v_ready = sem("v_ready")
        v_h = sem("v_h")
        v_l = sem("v_l")
        ln = {k: sem(f"ln_{k}") for k in ("mean", "cent", "sq", "sum", "var", "root", "inv", "spread", "scale", "scaled", "out")}
        ones_there = sem("ones_there")
        tab_in = sem("tab_in")
        vs_in = [sem(f"vs_in{b}") for b in range(2)]
        st_hi = sem("st_hi")
        st_lo = sem("st_lo")
        st_in = [[sem(f"st_in{b}_{e}") for e in range(2)] for b in range(2)]
        carried = sem("carried")
        s_rdy = sem("s_rdy")
        x_rdy = sem("x_rdy")
        p_rdy = sem("p_rdy")
        inv_rdy = sem("inv_rdy")
        pn_rdy = sem("pn_rdy")
        t_rdy = sem("t_rdy")
        pth_rdy = sem("pth_rdy")
        ptl_rdy = sem("ptl_rdy")
        pv_rdy = sem("pv_rdy")
        oh_rdy = sem("oh_rdy")
        o_rdy = sem("o_rdy")
        mix_hi = sem("mix_hi")
        mix_lo = sem("mix_lo")
        h_back = sem("h_back")
        wobank = sem("wobank")
        stored = sem("stored")

        def constants_there(eng):
            eng.wait_ge(c_in, 48)

        def add_squares(eng, ph, t):
            m = norms[ph]
            acc = rt[:, 2 + t, :]
            for d in range(1, DT):
                eng.wait_ge(m["sq"], 8 * t + d + 1)
                if d == 1:
                    eng.tensor_tensor(acc, tmp[:, 0, :], tmp[:, 1, :], ALU.add).then_inc(m["acc"], 1)
                else:
                    eng.wait_ge(m["acc"], 7 * t + d - 1)
                    eng.tensor_tensor(acc, acc, tmp[:, d % 2, :], ALU.add).then_inc(m["acc"], 1)

        block = ctx.enter_context(nc.Block())
        NU = 32
        LAG = 3

        V_BANKS = (4, 5, 7)
        CREDIT = 17

        def unit(n):
            g, r = (n % 16) // 4, n % 4
            return n // 16, 7 - g if r % 2 == 0 else g, 1 - r // 2

        def raw_scores(n):
            return flat(ps, 2 * (n % 2), (unit(n)[1] + 1) * P)

        def turned(n):
            return flat(ps, 3 + 2 * (n % 2), (unit(n)[1] + 1) * P).rearrange("p (j q) -> p j q", q=P)

        def block_of(m):
            return 4 * (m // 2) + 2 + m % 2

        @block.sync
        def _(sp):
            def load_unit(n, r):
                src = stream[ds(n, 1), :, :].rearrange("a p n -> p (a n)")
                sp.dma_start(wraw[:, r, :], src).then_inc(raw_in[r], 16)

            for t in range(2):
                for d in range(0, DT, 2):
                    sp.dma_start(h[:, d:d + 2, th(t)], xT[:, d:d + 2, th(t)]).then_inc(x_in[t][d // 2], 16)
                if t == 0:
                    sp.dma_start(cols[:, :], cols_in).then_inc(c_in, 16)
                    sp.dma_start(consts[:, :], smalls).then_inc(c_in, 16)
                    sp.dma_start(ident[:, :], ident_in).then_inc(c_in, 16)
                    for s in range(2):
                        load_unit(s, s)
            for s in range(2, 4):
                sp.wait_ge(w_lo[s - 2], 1)
                load_unit(s, s % 2)

            def ffn_loads(ph, first):
                f0, f45 = FILL[ph], FILL45[ph]
                with sp.Fori(0, CHUNKS) as i:
                    for s in (4, 5):
                        sp.wait_ge(w_lo[s - 2], i + (f0 + 1))
                        load_unit(i * 6 + (first + s), s % 2)
                    for s in range(4):
                        if s < 2:
                            sp.wait_ge(w_lo[s + 4], i + (f45 + 1))
                        else:
                            sp.wait_ge(w_lo[s - 2], i + (f0 + 2))
                        load_unit(i * 6 + (first + 6 + s), s % 2)

            def four_loads(ph, steps, first):
                f0 = FILL[ph]
                with sp.Fori(0, steps) as i:
                    for s in range(4):
                        sp.wait_ge(w_lo[(s + 2) % 4], i + (f0 + (1 if s < 2 else 2)))
                        load_unit(i * 4 + (first + 4 + s), s % 2)

            ffn_loads("ffn1", U_FFN1)
            for t in range(2):
                sp.wait_ge(dbank, 4 + 16 * (CHUNKS - 1) + 8 * (t + 1))
                sp.dma_start(h_spill.rearrange("p (d n) -> p d n", d=DT)[:, :, th(t)], h[:, :, th(t)]).then_inc(spilled, 16)
            four_loads("proj", PAIRS, U_PROJ)
            sp.wait_ge(qk_scale, PAIRS)
            sp.dma_start(table, table_in).then_inc(tab_in, 16)

            sp.wait_ge(v_l, 8)
            with sp.Fori(0, 2) as it:
                for b in range(2):
                    sp.wait_ge(st_lo, it * 4 + (2 * b + 2))
                    k0 = 4 * b
                    qh, ql, kh = xl[:, k0, :], xl[:, k0 + 1, :], xl[:, k0 + 2, :]
                    lo, hi = slice(0, DH), slice(DH, P)
                    for e, dst, src in (
                        (1, xh[hi, k0 + 1, :], qh[hi, :]), (1, xh[lo, k0 + 1, :], ql[hi, :]),
                        (1, xh[lo, k0 + 3, :], kh[hi, :]), (1, xh[hi, k0 + 3, :], kh[hi, :]),
                        (0, xh[lo, k0, :], qh[lo, :]), (0, xh[hi, k0, :], ql[lo, :]),
                        (0, xh[lo, k0 + 2, :], kh[lo, :]), (0, xh[hi, k0 + 2, :], kh[lo, :]),
                    ):
                        sp.dma_start(dst.bitcast(F32), src.bitcast(F32)).then_inc(st_in[b][e], 16)
                    sp.wait_ge(pv_rdy, it * NU + (16 * b + 1))
                    for dst, src in ((V_HI[b], v_hi), (V_LO[b], v_lo)):
                        for q in range(2):
                            sp.dma_start(
                                dst.bitcast(F32).rearrange("p (t c) -> p t c", c=P)[:, 4 * q:4 * q + 4, :],
                                src[q].bitcast(F32).rearrange("p (t c) -> p t c", c=HALF)[:, :, ds(it * (2 * P) + b * P, P)],
                            ).then_inc(vs_in[b], 16)
            for d in range(DT):
                sp.wait_ge(mix_lo, 8)
                sp.dma_start(h[:, d, :], h_spill[:, d * SEQ:(d + 1) * SEQ]).then_inc(h_back, 16)
            four_loads("wo", 4, U_WO)
            ffn_loads("ffn2", U_FFN2)
            for q in range(16):
                t, d = q // 8, q % 8
                sp.wait_ge(dbank, 4 + DUSE["ffn2"] + 16 * (CHUNKS - 1) + q + 1)
                sp.dma_start(outT[:, d, th(t)], h[:, d, th(t)]).then_inc(stored, 16)
            sp.wait_ge(stored, 256)

        @block.gpsimd
        def _(pool):
            pool.memset(glu[:, 0:TAPS - 1], 0.0).then_inc(glu_zero, 1)

            add_squares(pool, "ffn1", 1)
            for t in range(2):
                add_squares(pool, "proj", t)
            with pool.Fori(0, PAIRS) as i:
                for s in range(4):
                    pool.wait_ge(w_hi[s], i + (FILL["proj"] + 2))
                    pool.tensor_tensor(wl[:, s, :], wraw[:, s % 2, :], wh[:, s, :].bitcast(F32), ALU.subtract).then_inc(w_lo[s], 1)

            total = glu[:, 0:SEQ]
            for k in range(1, 4):
                pool.wait_ge(ln["sq"], k + 1)
                if k == 1:
                    pool.wait_ge(tapc, PAIRS * CHAIN + 1)
                    pool.tensor_tensor(total, wraw[:, 0, :], wraw[:, 1, :], ALU.add).then_inc(ln["sum"], 1)
                else:
                    pool.wait_ge(ln["sum"], k - 1)
                    pool.tensor_tensor(total, total, wraw[:, k % 2, :], ALU.add).then_inc(ln["sum"], 1)

            pool.wait_ge(qk_n, 4 * PAIRS)
            pool.wait_ge(done[3][1], FILL["v"] + 1)
            pool.wait_ge(st_lo, 2)
            for p in range(1, PAIRS):
                b = p % 2
                if p >= 2:
                    pool.wait_ge(pv_rdy, CREDIT + 16 * (p - 1))
                for which in range(2):
                    pool.tensor_copy(xl[:, 4 * b + 2 * which, :], h[:, 2 * p + which, :]).then_inc(st_hi, 1)
                for which in range(2):
                    pool.wait_ge(st_hi, 2 * p + which + 1)
                    pool.tensor_tensor(xl[:, 4 * b + 2 * which + 1, :], h[:, 2 * p + which, :],
                                       xl[:, 4 * b + 2 * which, :].bitcast(F32), ALU.subtract).then_inc(st_lo, 1)
            m = norms["ffn2"]
            for t in range(2):
                acc = rt[:, 2 + t, :]
                if t == 0:
                    pool.wait_ge(pn_rdy, 2 * NU)
                    pool.wait_ge(t_rdy, 2 * NU)
                pool.memset(acc, 0.0).then_inc(m["acc"], 1)
                with pool.Fori(0, 2) as i:
                    for s in range(4):
                        pool.wait_ge(m["acc"], i * 4 + (9 * t + s + 2))
                        pool.wait_ge(m["sq"], i * 4 + (8 * t + s + 1))
                        pool.tensor_tensor(acc, acc, tmp[:, s % 2, :], ALU.add).then_inc(m["acc"], 1)

        @block.scalar
        def _(act):
            def square(ph, t, d):
                m = norms[ph]
                if ph == "ffn1":
                    act.wait_ge(x_in[t][d // 2], 16)
                else:
                    act.wait_ge(dbank, 4 + 16 * (CHUNKS - 1) + 8 * t + d + 1)
                if t or d >= 2:
                    act.wait_ge(m["acc"], 7 * t + d - 2 if d > 2 else (7 * t + 1 if d == 2 else 7 * t))
                nc.scalar.activation(tmp[:, d % 2, :], h[:, d, th(t)], ACT.Square).then_inc(m["sq"], 1)

            def table_of_roots():
                act.wait_ge(eps_ready, 2)
                nc.scalar.activation(eps_col[:, 2:3], eps_col[:, 0:1], ACT.Sqrt).then_inc(dummy, 1)

            def scales(ph, t):
                m = norms[ph]
                act.wait_ge(m["stat"], t + 1)
                nc.scalar.activation(sm[:, 4 * t:4 * t + 4], ps[:, 2, 4 * t:4 * t + 4], ACT.Sqrt, bias=eps_col[:, 0:1]).then_inc(m["root"], 1)
                act.wait_ge(m["inv"], t + 1)
                nc.scalar.activation(rt[:, t, :].rearrange("p (b c) -> p b c", c=P),
                                     sm[:, 4 * t:4 * t + 4].unsqueeze(2).to_broadcast([P, 4, P]), ACT.Copy).then_inc(m["spread"], 1)

            def norm_hi(ph, q):
                m = norms[ph]
                act.wait_ge(m["xn"], q + 1)
                nc.scalar.activation(xh[:, q % 8, th(q // 8)], tmp[:, 2 + q % 2, :], ACT.Copy).then_inc(m["hi"], 1)

            def first_weights(s):
                act.wait_ge(raw_in[s % 2], 16 * (s // 2 + 1))
                nc.scalar.activation(wh[:, s, :], wraw[:, s % 2, :], ACT.Copy).then_inc(w_hi[s], 1)

            def ffn(ph):
                f0, f45, b0 = FILL[ph], FILL45[ph], BANKUSE[ph]
                u0 = {"ffn1": U_FFN1, "ffn2": U_FFN2}[ph]
                with act.Fori(0, CHUNKS) as i:
                    for f in range(2):
                        for t in range(2):
                            n = 2 * f + t
                            act.wait_ge(done[2 * f][t], i + (f0 - SKIPPED[ph][t] + 1))
                            act.wait_ge(ubank[t], i * 2 + (b0 + f + 1))
                            nc.scalar.activation(tmp[:, t, :], ps[:, 2 * t, :], ACT.Silu).then_inc(gbank[t], 1)
                            if n == 0:
                                for s in (4, 5):
                                    act.wait_ge(down_last, i + (f45 + 1))
                                    act.wait_ge(raw_in[s % 2], i * 48 + 16 * ((u0 + s) // 2 + 1))
                                    nc.scalar.activation(wh[:, s, :], wraw[:, s % 2, :], ACT.Copy).then_inc(w_hi[s], 1)
                            act.wait_ge(ubank[t], i * 2 + (b0 + f + 2))
                            nc.scalar.activation(ah[:, f, th(t)], tmp[:, 2 + t, :], ACT.Copy).then_inc(a_hi[t], 1)
                            if t == 1:
                                for s in (2 * f, 2 * f + 1):
                                    act.wait_ge(done[s][1], i + (f0 + 1))
                                    act.wait_ge(raw_in[s % 2], i * 48 + 16 * ((u0 + 6 + s) // 2 + 1))
                                    nc.scalar.activation(wh[:, s, :], wraw[:, s % 2, :], ACT.Copy).then_inc(w_hi[s], 1)

            act.sem_inc(down_last, 1)
            for t in range(2):
                act.sem_inc(ubank[t], 1)
            table_of_roots()
            for d in range(DT):
                square("ffn1", 0, d)
            scales("ffn1", 0)
            first_weights(0)
            first_weights(1)
            for q in range(8):
                norm_hi("ffn1", q)
                square("ffn1", 1, q)
            first_weights(2)
            first_weights(3)
            scales("ffn1", 1)
            for q in range(8, 16):
                norm_hi("ffn1", q)
            ffn("ffn1")
            table_of_roots()
            for t in range(2):
                for d in range(DT):
                    square("proj", t, d)
            scales("proj", 0)
            for q in range(16):
                if q == 8:
                    scales("proj", 1)
                norm_hi("proj", q)

            f0, b0 = FILL["proj"], BANKUSE["proj"]
            act.wait_ge(spilled, 32)
            with act.Fori(0, PAIRS) as i:
                for t in range(2):
                    act.wait_ge(done[0][t], i + (f0 + 1))
                    act.wait_ge(ubank[t], i * 2 + (b0 + 1))
                    nc.scalar.activation(tmp[:, t, :], ps[:, 2 * t, :], ACT.Sigmoid).then_inc(gbank[t], 1)
                for s in (0, 1):
                    act.wait_ge(done[s][1], i + (f0 + 1))
                    act.wait_ge(raw_in[s % 2], i * 32 + 16 * ((U_PROJ + 4 + s) // 2 + 1))
                    nc.scalar.activation(wh[:, s, :], wraw[:, s % 2, :], ACT.Copy).then_inc(w_hi[s], 1)
                for t in range(2):
                    constants_there(act)
                    act.wait_ge(done[2][t], i + (f0 + 1))
                    nc.scalar.activation(h[:, ds(i * 2, 1), th(t)].rearrange("p a n -> p (a n)"), ps[:, 2 * t, :], ACT.Copy).then_inc(gbank[t], 1)
                    constants_there(act)
                    act.wait_ge(done[3][t], i + (f0 + 1))
                    nc.scalar.activation(h[:, ds(i * 2 + 1, 1), th(t)].rearrange("p a n -> p (a n)"), ps[:, 2 * t + 1, :], ACT.Copy).then_inc(ubank[t], 1)
                for s in (2, 3):
                    act.wait_ge(done[s][1], i + (f0 + 1))
                    act.wait_ge(raw_in[s % 2], i * 32 + 16 * ((U_PROJ + 4 + s) // 2 + 1))
                    nc.scalar.activation(wh[:, s, :], wraw[:, s % 2, :], ACT.Copy).then_inc(w_hi[s], 1)

            def v_out(tt):
                if tt in (3, 7):
                    act.wait_ge(done[3][tt // 4], FILL["v"] + 1)
                else:
                    act.wait_ge(v_ready, tt + 1 - (tt > 3))
                nc.scalar.activation(v_hi[tt // 4][:, (tt % 4) * 512:(tt % 4 + 1) * 512], ps[:, V_BANKS[tt % 3], :], ACT.Copy).then_inc(v_h, 1)

            def qk_squares(j):
                if j == 0:
                    for t in range(2):
                        act.wait_ge(ubank[t], b0 + 2 * PAIRS + 1)
                if j >= 1:
                    act.wait_ge(qk_stat, j)
                for which in range(2):
                    nc.scalar.activation(flat(tmp, 2 * which, 1024), h[:, 2 * j + which, :], ACT.Square).then_inc(qk_sq, 1)

            def qk_root(j):
                act.wait_ge(qk_stat, j + 1)
                nc.scalar.activation(sm[:, 32 * j:32 * j + 32], ps[:, 6, 32 * j:32 * j + 32], ACT.Sqrt, bias=eps_col[:, 0:1]).then_inc(qk_rooted, 1)

            def qk_spreads(j):
                act.wait_ge(qk_inv, j + 1)
                if j == 0:
                    act.wait_ge(tapc, PAIRS * CHAIN + 1)
                if j >= 1:
                    act.wait_ge(qk_scale, j)
                nc.scalar.activation(flat(rt, 0, 2048).rearrange("p (b c) -> p b c", c=DH),
                                     sm[:, 32 * j:32 * j + 32].unsqueeze(2).to_broadcast([P, 32, DH]), ACT.Copy).then_inc(qk_spread, 1)

            qk_squares(0)
            v_out(0)
            v_out(1)
            for s in (2, 3):
                act.wait_ge(w_lo[s], FILL["v"] + 1)
            for k in range(4):
                act.wait_ge(ln["cent"], 8 if k == 3 else k + 5)
                if k >= 2:
                    act.wait_ge(ln["sum"], 1)
                nc.scalar.activation(wraw[:, k % 2, :], y[:, k, :], ACT.Square).then_inc(ln["sq"], 1)
            v_out(2)
            v_out(3)
            act.wait_ge(ln["var"], 1)
            nc.scalar.activation(sm[:, 128:136], ps[:, 6, 128:136], ACT.Sqrt, bias=eps_col[:, 0:1]).then_inc(ln["root"], 1)
            act.wait_ge(ln["inv"], 1)
            nc.scalar.activation(wraw[:, 0, :].rearrange("p (b c) -> p b c", c=P),
                                 sm[:, 128:136].unsqueeze(2).to_broadcast([P, 8, P]), ACT.Copy).then_inc(ln["spread"], 1)
            for j in range(PAIRS):
                qk_root(j)
                qk_spreads(j)
                v_out(4 + j)
                if j + 1 < PAIRS:
                    qk_squares(j + 1)

            act.wait_ge(done[3][1], FILL["v"] + 1)
            for which in range(2):
                nc.scalar.activation(xl[:, 2 * which, :], h[:, which, :], ACT.Copy).then_inc(st_hi, 1)
            act.wait_ge(ln["scaled"], 8)
            for k in range(4):
                nc.scalar.activation(y[:, k, :], y[:, k, :], ACT.Silu, bias=consts[:, C_LB + k:C_LB + k + 1]).then_inc(ln["out"], 1)

            with act.Fori(0, 2) as it:
                def probs_hi(n):
                    b, i, e = unit(n)
                    act.wait_ge(t_rdy, it * NU + (n + 1))
                    if n >= 4:
                        act.wait_ge(pv_rdy, it * NU + (CREDIT + n - 3))
                    nc.scalar.activation(probs(n)[:, 0:i + 1, 0, :], turned(n), ACT.Copy).then_inc(pth_rdy, 1)

                def out_half(m):
                    n = block_of(m)
                    act.wait_ge(pv_rdy, it * NU + (CREDIT + n + 1))
                    for e in range(2):
                        nc.scalar.activation(glu[DH * e:DH * e + DH, (m % 2) * P:(m % 2 + 1) * P],
                                             ps[DH * e:DH * e + DH, 6 + m % 2, 2 * P * e:2 * P * e + P], ACT.Copy).then_inc(oh_rdy, 1)

                for n in range(NU + LAG + 2):
                    if LAG <= n < NU + LAG:
                        probs_hi(n - LAG)
                    if n < NU:
                        b, i, e = unit(n)
                        nk = (i + 1) * P
                        act.wait_ge(x_rdy, it * NU + (n + 1))
                        nc.scalar.activation(scores[n % 4][:, 0:nk], scores[n % 4][:, 0:nk], ACT.Exp, bias=negmax[:, n:n + 1],
                                             scale=-1.0, accum_out=rowsum[:, n:n + 1]).then_inc(p_rdy, 1)
                    k = n - LAG - 2
                    if k >= 0 and k % 4 >= 2:
                        out_half(2 * (k // 4) + k % 2)

            act.wait_ge(ptl_rdy, 2 * NU)
            act.wait_ge(pv_rdy, 2 * NU + CREDIT)
            for s in range(2):
                act.dma_start(wraw[:, s, :], stream[U_WO + s, :, :]).then_inc(raw_in[s], 16)

            def wo_unit(s):
                act.wait_ge(raw_in[s % 2], 16 * ((U_WO + s) // 2 + 1))
                nc.scalar.activation(wh[:, s, :], wraw[:, s % 2, :], ACT.Copy).then_inc(w_hi[s], 1)

            def mix(m):
                act.wait_ge(o_rdy, 64)
                src = h[:, 2 * m, :] if m < 4 else y[:, m - 4, :]
                nc.scalar.activation(xh[:, m, :], src, ACT.Copy).then_inc(mix_hi, 1)

            for m in range(DT):
                if m == 2:
                    wo_unit(0)
                    wo_unit(1)
                mix(m)
            for s in (2, 3):
                act.wait_ge(w_lo[s - 2], FILL["wo"] + 1)
                act.dma_start(wraw[:, s % 2, :], stream[U_WO + s, :, :]).then_inc(raw_in[s % 2], 16)
                wo_unit(s)
            table_of_roots()
            m = norms["ffn2"]
            act.sem_inc(m["acc"], 1)
            def wo_step(i, s, t):
                f0 = FILL["wo"] + 2 * t
                act.wait_ge(done[s][1], i + (f0 + 1))
                act.wait_ge(raw_in[s % 2], i * 32 + 16 * ((U_WO + 8 * t + 4 + s) // 2 + 1))
                nc.scalar.activation(wh[:, s, :], wraw[:, s % 2, :], ACT.Copy).then_inc(w_hi[s], 1)
                act.wait_ge(m["acc"], i * 4 + (9 * t + s + 1))
                constants_there(act)
                act.wait_ge(wobank, i * 4 + (4 + 8 * t + s + 1))
                nc.scalar.activation(tmp[:, s % 2, :], h[:, ds(i * 4 + s, 1), th(t)].rearrange("p a n -> p (a n)"),
                                     ACT.Square).then_inc(m["sq"], 1)

            with act.Fori(0, 2) as i:
                for s in range(4):
                    wo_step(i, s, 0)
            for u in range(DT):
                if u == 0:
                    scales("ffn2", 0)
                if u < 4:
                    norm_hi("ffn2", 2 * u)
                    norm_hi("ffn2", 2 * u + 1)
                wo_step(u // 4, u % 4, 1)
            scales("ffn2", 1)
            for q in range(8, 16):
                norm_hi("ffn2", q)
            ffn("ffn2")

        @block.vector
        def _(dve):
            def lo_part(s, value):
                dve.wait_ge(w_hi[s], value)
                nc.vector.tensor_tensor(wl[:, s, :], wraw[:, s % 2, :], wh[:, s, :].bitcast(F32), ALU.subtract).then_inc(w_lo[s], 1)

            def inverse(ph, t):
                m = norms[ph]
                dve.wait_ge(m["root"], t + 1)
                nc.vector.reciprocal(sm[:, 4 * t:4 * t + 4], sm[:, 4 * t:4 * t + 4]).then_inc(m["inv"], 1)

            def norm(ph, first, last):
                m = norms[ph]
                for q in range(first, last + 1):
                    if q < last:
                        t, d = q // 8, q % 8
                        dve.wait_ge(m["scale"], t + 1)
                        if q >= 2:
                            dve.wait_ge(m[f"lo{(q - 2) // 8}"], (q - 2) % 8 + 1)
                        g = C_G[ph] + d
                        nc.vector.scalar_tensor_tensor(out=tmp[:, 2 + d % 2, :], in0=h[:, d, th(t)], scalar=consts[:, g:g + 1],
                                                       in1=ps[:, 3 + 4 * t, :], op0=ALU.mult, op1=ALU.mult).then_inc(m["xn"], 1)
                    if q > first:
                        t, d = (q - 1) // 8, (q - 1) % 8
                        dve.wait_ge(m["hi"], q)
                        nc.vector.tensor_tensor(xl[:, d, th(t)], tmp[:, 2 + d % 2, :], xh[:, d, th(t)].bitcast(F32),
                                                ALU.subtract).then_inc(m[f"lo{t}"], 1)
                if last == 16:
                    dve.wait_ge(m["lo1"], 8)

            def ffn(ph):
                f0, f45, b0, d0 = FILL[ph], FILL45[ph], BANKUSE[ph], DUSE[ph]
                with dve.Fori(0, CHUNKS) as i:
                    def gated(f, t):
                        dve.wait_ge(gbank[t], i * 2 + (b0 + f + 2))
                        dve.wait_ge(done[2 * f + 1][t], i + (f0 - SKIPPED[ph][t] + 1))
                        nc.vector.tensor_tensor(tmp[:, 2 + t, :], tmp[:, t, :], ps[:, 2 * t + 1, :], ALU.mult).then_inc(ubank[t], 1)
                        dve.wait_ge(a_hi[t], i * 2 + (b_ffn + f + 1))
                        nc.vector.tensor_tensor(al[:, f, th(t)], tmp[:, 2 + t, :], ah[:, f, th(t)].bitcast(F32),
                                                ALU.subtract).then_inc(a_lo[t], 1)

                    def add_down(q):
                        t, d = q // 8, q % 8
                        if q == 15:
                            dve.wait_ge(down_last, i + (f45 + 2))
                        else:
                            dve.wait_ge(down, i * 15 + (15 * d0 // 16 + q + 1))
                        nc.vector.scalar_tensor_tensor(out=h[:, d, th(t)], in0=ps[:, 4 + q % 4, :], scalar=0.5,
                                                       in1=h[:, d, th(t)], op0=ALU.mult, op1=ALU.add).then_inc(dbank, 1)

                    b_ffn = {"ffn1": 0, "ffn2": 2 * CHUNKS}[ph]
                    gated(0, 0)
                    lo_part(4, i + (f45 + 1))
                    lo_part(5, i + (f45 + 1))
                    gated(0, 1)
                    lo_part(0, i + (f0 + 2))
                    lo_part(1, i + (f0 + 2))
                    gated(1, 0)
                    gated(1, 1)
                    for q in range(16):
                        add_down(q)
                        if q == 3:
                            lo_part(2, i + (f0 + 2))
                            lo_part(3, i + (f0 + 2))

            dve.sem_inc(tapc, 1)
            nc.vector.memset(ones[:, :], 1.0 / 512).then_inc(ones_there, 1)
            nc.vector.memset(eps_col[:, 0:1], EPS).then_inc(eps_ready, 1)
            nc.vector.memset(eps_col[:, 1:2], 64 * EPS).then_inc(eps_ready, 1)
            add_squares(dve, "ffn1", 0)
            inverse("ffn1", 0)
            lo_part(0, 1)
            lo_part(1, 1)
            dve.wait_ge(c_in, 48)
            norm("ffn1", 0, 8)
            lo_part(2, 1)
            lo_part(3, 1)
            inverse("ffn1", 1)
            norm("ffn1", 8, 16)
            nc.vector.tensor_scalar(negqg[:, :], consts[:, C_QG:C_QG + 1], -0.125, None, ALU.mult).then_inc(qg_neg, 1)
            ffn("ffn1")
            for t in range(2):
                inverse("proj", t)
                norm("proj", 8 * t, 8 * t + 8)

            f0, b0 = FILL["proj"], BANKUSE["proj"]
            dve.wait_ge(qg_neg, 1)
            dve.wait_ge(glu_zero, 1)
            with dve.Fori(0, PAIRS) as i:
                dve.wait_ge(tapc, i * CHAIN + 1)
                for t in range(2):
                    dve.wait_ge(gbank[t], i * 2 + (b0 + 2))
                    dve.wait_ge(done[1][t], i + (f0 + 1))
                    nc.vector.tensor_tensor(glu[:, TAPS - 1 + t * HALF:TAPS - 1 + (t + 1) * HALF], tmp[:, t, :], ps[:, 2 * t + 1, :],
                                            ALU.mult).then_inc(ubank[t], 1)
                ytile = y[:, ds(i, 1), :].rearrange("p a n -> p (a n)")
                odd = flat(rt, 0, SEQ)
                for k in range(TAPS):
                    if k == 0:
                        dve.wait_ge(ubank[1], i * 2 + (b0 + 2))
                        nc.vector.tensor_scalar(ytile, glu[:, 0:SEQ], consts[:, ds(i * TAPS + C_CW, 1)], consts[:, ds(i + C_CB, 1)],
                                                ALU.mult, ALU.add).then_inc(tapc, 1)
                    elif k == 1:
                        nc.vector.tensor_scalar(odd, glu[:, 1:1 + SEQ], consts[:, ds(i * TAPS + (C_CW + 1), 1)], None,
                                                ALU.mult).then_inc(tapc, 1)
                    else:
                        total = odd if k % 2 else ytile
                        dve.wait_ge(tapc, i * CHAIN + k)
                        nc.vector.scalar_tensor_tensor(out=total, in0=glu[:, k:k + SEQ], scalar=consts[:, ds(i * TAPS + (C_CW + k), 1)],
                                                       in1=total, op0=ALU.mult, op1=ALU.add).then_inc(tapc, 1)
                dve.wait_ge(tapc, i * CHAIN + (TAPS + 1))
                nc.vector.tensor_tensor(ytile, ytile, odd, ALU.add).then_inc(tapc, 1)

            def v_out(tt):
                dve.wait_ge(v_h, tt + 1)
                c = slice((tt % 4) * 512, (tt % 4 + 1) * 512)
                nc.vector.tensor_tensor(v_lo[tt // 4][:, c], ps[:, V_BANKS[tt % 3], :], v_hi[tt // 4][:, c].bitcast(F32),
                                        ALU.subtract).then_inc(v_l, 1)

            def qk_inverse(j):
                dve.wait_ge(qk_rooted, j + 1)
                nc.vector.reciprocal(sm[:, 32 * j:32 * j + 32], sm[:, 32 * j:32 * j + 32]).then_inc(qk_inv, 1)

            def qk_scaled(j):
                dve.wait_ge(qk_scale, j + 1)
                for n in range(4):
                    tile = h[:, 2 * j + n // 2, th(n % 2)]
                    gain = consts[:, C_KG:C_KG + 1] if n >= 2 else negqg[:, 0:1]
                    nc.vector.scalar_tensor_tensor(out=tile, in0=tile, scalar=gain, in1=ps[:, n, :], op0=ALU.mult,
                                                   op1=ALU.mult).then_inc(qk_n, 1)

            v_out(0)
            v_out(1)
            for t in range(2):
                for k in range(4):
                    dve.wait_ge(ln["mean"], t + 1)
                    nc.vector.tensor_tensor(y[:, k, th(t)], y[:, k, th(t)], ps[:, t, :], ALU.subtract).then_inc(ln["cent"], 1)
            v_out(2)
            v_out(3)
            dve.wait_ge(ln["root"], 1)
            nc.vector.reciprocal(sm[:, 128:136], sm[:, 128:136]).then_inc(ln["inv"], 1)
            dve.wait_ge(ln["scale"], 2)
            for k in range(4):
                for t in range(2):
                    nc.vector.scalar_tensor_tensor(out=y[:, k, th(t)], in0=y[:, k, th(t)], scalar=consts[:, C_LG + k:C_LG + k + 1],
                                                   in1=ps[:, 2 + t, :], op0=ALU.mult, op1=ALU.mult).then_inc(ln["scaled"], 1)
            for j in range(PAIRS):
                qk_inverse(j)
                v_out(4 + j)
                if j == PAIRS - 1:
                    for which in range(2):
                        dve.wait_ge(st_hi, which + 1)
                        nc.vector.tensor_tensor(xl[:, 2 * which + 1, :], h[:, which, :], xl[:, 2 * which, :].bitcast(F32),
                                                ALU.subtract).then_inc(st_lo, 1)
                qk_scaled(j)

            dve.wait_ge(tab_in, 16)
            with dve.Fori(0, 2) as it:
                def masked(n):
                    b, i, e = unit(n)
                    nk = (i + 1) * P
                    if n < 2:
                        dve.wait_ge(s_rdy, it * NU + (CREDIT + n + 1))
                        nc.vector.memset(rowinv[:, n:n + 1], 0.0).then_inc(carried, 1)
                    nc.vector.tensor_tensor_reduce(scores[n % 4][:, 0:nk], raw_scores(n), table[:, SEQ - nk:SEQ], 1.0, 3e38,
                                                   ALU.add, ALU.min, negmax[:, n:n + 1]).then_inc(x_rdy, 1)

                def normalised(n):
                    b, i, e = unit(n)
                    nk = (i + 1) * P
                    dve.wait_ge(p_rdy, it * NU + (n + 1))
                    nc.vector.reciprocal(rowinv[:, n:n + 1], rowsum[:, n:n + 1]).then_inc(inv_rdy, 1)
                    dve.wait_ge(inv_rdy, it * NU + (n + 1))
                    if n + 2 < NU:
                        dve.wait_ge(s_rdy, it * NU + (CREDIT + n + 3))
                    nc.vector.tensor_scalar(scores[n % 4][:, 0:nk], scores[n % 4][:, 0:nk], rowinv[:, n:n + 1], None,
                                            ALU.mult).then_inc(pn_rdy, 1)

                def probs_lo(n):
                    b, i, e = unit(n)
                    dve.wait_ge(pth_rdy, it * NU + (n + 1))
                    nc.vector.tensor_tensor(probs(n)[:, 0:i + 1, 1, :], turned(n), probs(n)[:, 0:i + 1, 0, :].bitcast(F32),
                                            ALU.subtract).then_inc(ptl_rdy, 1)

                def heads_out(m):
                    b, i, e = unit(block_of(m))
                    for e in range(2):
                        rows = slice(DH * e, DH * e + DH)
                        dve.wait_ge(oh_rdy, it * NU + (2 * m + e + 1))
                        nc.vector.tensor_tensor(h[rows, ds(it * 4 + 2 * b, 1), i * P:(i + 1) * P].rearrange("p a n -> p (a n)"),
                                                ps[rows, 6 + m % 2, 2 * P * e + P:2 * P * e + 2 * P],
                                                glu[rows, (m % 2) * P:(m % 2 + 1) * P], ALU.add).then_inc(o_rdy, 1)

                for n in range(NU + LAG + 2):
                    if n < NU:
                        masked(n)
                    if 1 <= n <= NU:
                        normalised(n - 1)
                    if LAG <= n < NU + LAG:
                        probs_lo(n - LAG)
                    k = n - LAG - 2
                    if k >= 0 and k % 4 >= 2:
                        heads_out(2 * (k // 4) + k % 2)

            def mix(m):
                dve.wait_ge(mix_hi, m + 1)
                src = h[:, 2 * m, :] if m < 4 else y[:, m - 4, :]
                nc.vector.tensor_tensor(xl[:, m, :], src, xh[:, m, :].bitcast(F32), ALU.subtract).then_inc(mix_lo, 1)

            f0 = FILL["wo"]
            for m in range(DT):
                if m == 2:
                    lo_part(0, f0 + 1)
                    lo_part(1, f0 + 1)
                mix(m)
            for s in (2, 3):
                lo_part(s, f0 + 1)
            def wo_step(i, s, t):
                f0 = FILL["wo"] + 2 * t
                dve.wait_ge(done[s][1], i + (f0 + 1))
                dve.wait_ge(h_back, 16 * DT)
                tile = h[:, ds(i * 4 + s, 1), th(t)].rearrange("p a n -> p (a n)")
                nc.vector.tensor_tensor(tile, ps[:, 4 + s, :], tile, ALU.add).then_inc(wobank, 1)
                lo_part(s, i + (f0 + 2))

            with dve.Fori(0, 2) as i:
                for s in range(4):
                    wo_step(i, s, 0)
            for u in range(DT):
                if u == 0:
                    inverse("ffn2", 0)
                if u < 4:
                    norm("ffn2", 2 * u, 2 * u + 2)
                wo_step(u // 4, u % 4, 1)
            inverse("ffn2", 1)
            norm("ffn2", 8, 16)
            ffn("ffn2")

        @block.tensor
        def _(pe):
            def three(out, lhs_hi, lhs_lo, rhs_hi, rhs_lo, start, stop):
                nc.tensor.matmul(out, lhs_hi, rhs_hi, start=start, stop=False)
                nc.tensor.matmul(out, lhs_hi, rhs_lo, start=False, stop=False)
                return nc.tensor.matmul(out, lhs_lo, rhs_hi, start=False, stop=stop)

            def turn_scales(bank, spread, blocks):
                for b in range(blocks):
                    mm = nc.tensor.transpose(ps[:, bank + b // 4, (b % 4) * P:(b % 4 + 1) * P], spread[:, b * P:(b + 1) * P], ident[:, :])
                return mm

            def norm_stats(ph, t):
                m = norms[ph]
                pe.wait_ge(m["acc"], SUMMED[ph][t])
                for b in range(4):
                    mm = nc.tensor.matmul(ps[:, 2, 4 * t + b:4 * t + b + 1], rt[:, 2 + t, b * P:(b + 1) * P], cols[:, 0:1],
                                          start=True, stop=True)
                mm.then_inc(m["stat"], 1)

            def norm_scales(ph, t):
                m = norms[ph]
                pe.wait_ge(m["spread"], t + 1)
                turn_scales(3 + 4 * t, rt[:, t, :], 4).then_inc(m["scale"], 1)

            def column(bank, s, t, ready=None):
                for d in range(DT):
                    if ready is not None:
                        pe.wait_ge(ready, d + 1)
                    c = slice(d * P, (d + 1) * P)
                    mm = three(ps[:, bank, :], wh[:, s, c], wl[:, s, c], xh[:, d, th(t)], xl[:, d, th(t)], d == 0, d == DT - 1)
                return mm

            def two_columns(t, ready):
                for d in range(DT):
                    pe.wait_ge(ready, d + 1)
                    c = slice(d * P, (d + 1) * P)
                    for s in range(2):
                        mm = three(ps[:, 2 * t + s, :], wh[:, s, c], wl[:, s, c], xh[:, d, th(t)], xl[:, d, th(t)], d == 0, d == DT - 1)
                        if d == DT - 1:
                            mm.then_inc(done[s][t], 1)

            def ffn(ph):
                f0, f45, b0, d0 = FILL[ph], FILL45[ph], BANKUSE[ph], DUSE[ph]
                b_ffn = {"ffn1": 0, "ffn2": 2 * CHUNKS}[ph]

                def chunk(i, k):
                    first = k == 0
                    for f in range(2):
                        for t in range(2):
                            if first and f == 0 and t == 1:
                                norm_stats(ph, 1)
                                norm_scales(ph, 1)
                            pe.wait_ge(gbank[t], i * 2 + (b0 + 2 * k + f + 1))
                            if first and f == 0:
                                pe.wait_ge(ubank[t], b0 + 1)
                                pe.wait_ge(w_lo[0], f0 + 1)
                                pe.wait_ge(w_lo[1], f0 + 1)
                                two_columns(t, norms[ph][f"lo{t}"])
                                continue
                            if t == 0:
                                pe.wait_ge(w_lo[2 * f], i + (f0 + k + 1))
                            column(2 * t, 2 * f, t).then_inc(done[2 * f][t], 1)
                            pe.wait_ge(ubank[t], i * 2 + (b0 + 2 * k + f + 1))
                            if t == 0:
                                pe.wait_ge(w_lo[2 * f + 1], i + (f0 + k + 1))
                            column(2 * t + 1, 2 * f + 1, t).then_inc(done[2 * f + 1][t], 1)
                    for q in range(16):
                        t, d = q // 8, q % 8
                        if q == 0:
                            pe.wait_ge(w_lo[4], i + (f45 + k + 1))
                            pe.wait_ge(w_lo[5], i + (f45 + k + 1))
                        if d == 0:
                            pe.wait_ge(a_lo[t], i * 2 + (b_ffn + 2 * k + 2))
                        pe.wait_ge(dbank, i * 16 + (d0 + 16 * k + q + 1))
                        c = slice(d * P, (d + 1) * P)
                        for f in range(2):
                            mm = three(ps[:, 4 + q % 4, :], wh[:, 4 + f, c], wl[:, 4 + f, c], ah[:, f, th(t)], al[:, f, th(t)], f == 0, f == 1)
                        mm.then_inc(down_last if q == 15 else down, 1)

                chunk(0, 0)
                with pe.Fori(0, CHUNKS - 1) as i:
                    chunk(i, 1)

            for t in range(2):
                pe.sem_inc(gbank[t], 1)
            pe.sem_inc(dbank, 4)
            pe.sem_inc(wobank, 4)
            pe.sem_inc(pv_rdy, CREDIT)
            pe.sem_inc(s_rdy, CREDIT)
            pe.wait_ge(c_in, 48)
            norm_stats("ffn1", 0)
            norm_scales("ffn1", 0)
            ffn("ffn1")
            norm_stats("proj", 0)
            norm_scales("proj", 0)
            f0, b0 = FILL["proj"], BANKUSE["proj"]

            def projections(i, k):
                first = k == 0
                for part in range(2):
                    for t in range(2):
                        if first and part == 0 and t == 1:
                            norm_stats("proj", 1)
                            norm_scales("proj", 1)
                        pe.wait_ge(gbank[t], i * 2 + (b0 + 2 * k + part + 1))
                        if first and part == 0:
                            pe.wait_ge(ubank[t], b0 + 1)
                            pe.wait_ge(w_lo[0], f0 + 1)
                            pe.wait_ge(w_lo[1], f0 + 1)
                            two_columns(t, norms["proj"][f"lo{t}"])
                            continue
                        if t == 0:
                            pe.wait_ge(w_lo[2 * part], i + (f0 + k + 1))
                        column(2 * t, 2 * part, t).then_inc(done[2 * part][t], 1)
                        pe.wait_ge(ubank[t], i * 2 + (b0 + 2 * k + part + 1))
                        if t == 0:
                            pe.wait_ge(w_lo[2 * part + 1], i + (f0 + k + 1))
                        column(2 * t + 1, 2 * part + 1, t).then_inc(done[2 * part + 1][t], 1)

            projections(0, 0)
            with pe.Fori(0, PAIRS - 1) as i:
                projections(i, 1)

            def v_rows(tt):
                if tt >= 3:
                    pe.wait_ge(v_l, tt - 2)
                for d in range(DT):
                    s, r = d // 2, d % 2
                    if tt == 0 and r == 0:
                        pe.wait_ge(w_lo[s], FILL["v"] + 1)
                    c = slice(tt * P, (tt + 1) * P)
                    w = slice(r * 512, (r + 1) * 512)
                    mm = three(ps[:, V_BANKS[tt % 3], :], xh[:, d, c], xl[:, d, c], wh[:, s, w], wl[:, s, w], d == 0, d == DT - 1)
                    if tt in (3, 7) and r == 1:
                        mm.then_inc(done[s][tt // 4], 1)
                if tt not in (3, 7):
                    mm.then_inc(v_ready, 1)

            def qk_stats(j):
                pe.wait_ge(qk_sq, 2 * j + 2)
                for n in range(16):
                    mm = nc.tensor.matmul(ps[:, 6, 32 * j + 2 * n:32 * j + 2 * n + 2], flat(tmp, 0, 2048)[:, n * P:(n + 1) * P],
                                          cols[:, 1:3], start=True, stop=True)
                mm.then_inc(qk_stat, 1)

            def qk_turn(j):
                pe.wait_ge(qk_spread, j + 1)
                if j >= 1:
                    pe.wait_ge(qk_n, 4 * j)
                turn_scales(0, flat(rt, 0, 2048), 16).then_inc(qk_scale, 1)

            def ln_mean():
                pe.wait_ge(ones_there, 1)
                pe.wait_ge(tapc, PAIRS * CHAIN + 1)
                for t in range(2):
                    pe.wait_ge(gbank[t], b0 + 2 * PAIRS + 1)
                    pe.wait_ge(ubank[t], b0 + 2 * PAIRS + 1)
                for t in range(2):
                    for k in range(4):
                        mm = nc.tensor.matmul(ps[:, t, :], ones[:, :], y[:, k, th(t)], start=(k == 0), stop=(k == 3))
                    mm.then_inc(ln["mean"], 1)

            def ln_var():
                pe.wait_ge(ln["sum"], 3)
                for b in range(8):
                    mm = nc.tensor.matmul(ps[:, 6, 128 + b:129 + b], glu[:, b * P:(b + 1) * P], cols[:, 3:4], start=True, stop=True)
                mm.then_inc(ln["var"], 1)

            v_rows(0)
            v_rows(1)
            v_rows(2)
            ln_mean()
            v_rows(3)
            ln_var()
            v_rows(4)
            pe.wait_ge(ln["spread"], 1)
            for t in range(2):
                turn_scales(2 + t, wraw[:, 0, th(t)], 4).then_inc(ln["scale"], 1)
            qk_stats(0)
            for j in range(PAIRS):
                if j < PAIRS - 1:
                    v_rows(5 + j)
                if j == 0:
                    pe.wait_ge(ln["scaled"], 8)
                qk_turn(j)
                if j + 1 < PAIRS:
                    qk_stats(j + 1)

            pe.wait_ge(qk_n, 4 * PAIRS)
            with pe.Fori(0, 2) as it:
                def score(n):
                    b, i, e = unit(n)
                    if n % 16 in (0, 2):
                        pe.wait_ge(st_in[b][e], it * 64 + 64)
                    if n >= 2:
                        pe.wait_ge(x_rdy, it * NU + (n - 1))
                    nk = (i + 1) * P
                    rows = slice(DH * e, DH * e + DH)
                    q = slice(i * P, (i + 1) * P)
                    for c in range(0, nk, 512):
                        w = min(512, nk - c)
                        out = ps[:, 2 * (n % 2) + c // 512, 0:w]
                        nc.tensor.matmul(out, xh[:, 4 * b + e, q], xh[:, 4 * b + 2 + e, c:c + w], start=True, stop=False)
                        mm = nc.tensor.matmul(out, xl[rows, 4 * b, q], xl[rows, 4 * b + 3, c:c + w], start=False, stop=True)
                    mm.then_inc(s_rdy, 1)

                def turn(n):
                    b, i, e = unit(n)
                    pe.wait_ge(pn_rdy, it * NU + (n + 1))
                    if n >= 2:
                        pe.wait_ge(ptl_rdy, it * NU + (n - 1))
                    for j in range(i + 1):
                        mm = nc.tensor.transpose(ps[:, 3 + 2 * (n % 2) + j // 4, (j % 4) * P:(j % 4 + 1) * P], scores[n % 4][:, j * P:(j + 1) * P],
                                                 ident[:, :])
                    mm.then_inc(t_rdy, 1)

                def weighted(n):
                    b, i, e = unit(n)
                    m = 2 * (n // 4) + n % 2
                    if n % 16 == 0:
                        pe.wait_ge(vs_in[b], it * 64 + 64)
                    pe.wait_ge(ptl_rdy, it * NU + (n + 1))
                    if e == 1 and m >= 2:
                        pe.wait_ge(o_rdy, it * NU + 2 * (m - 1))
                    out = ps[:, 6 + m % 2, 2 * P * e:2 * P * e + 2 * P]
                    for j in range(i + 1):
                        c = slice(j * P, (j + 1) * P)
                        both = probs(n)[:, j, :, :].rearrange("p a q -> p (a q)")
                        nc.tensor.matmul(out, V_HI[b][:, c], both, start=j == 0, stop=False)
                        mm = nc.tensor.matmul(out, V_LO[b][:, c], both, start=False, stop=j == i)
                    mm.then_inc(pv_rdy, 1)

                score(0)
                score(1)
                for n in range(NU + LAG + 1):
                    if n > LAG:
                        weighted(n - LAG - 1)
                    if n + 2 < NU:
                        score(n + 2)
                    if 1 <= n <= NU:
                        turn(n - 1)

            f0 = FILL["wo"]
            pe.wait_ge(o_rdy, 64)

            def wo_unit(i, s, t):
                pe.wait_ge(w_lo[s], i + (f0 + 2 * t + 1))
                pe.wait_ge(wobank, i * 4 + (8 * t + s + 1))
                column(4 + s, s, t, mix_lo if t == 0 and s == 0 else None).then_inc(done[s][1], 1)

            with pe.Fori(0, 2) as i:
                for s in range(4):
                    wo_unit(i, s, 0)
            for u in range(DT):
                wo_unit(u // 4, u % 4, 1)
                if u == 0:
                    norm_stats("ffn2", 0)
                elif u == 1:
                    norm_scales("ffn2", 0)
            ffn("ffn2")


def kernel(**inputs):
    import numpy as np
    import concourse.bacc as bacc
    from concourse.bass_utils import run_bass_kernel_spmd

    w = {k: np.asarray(v) for k, v in inputs.items()}

    def columns(m):
        return m.reshape(DT, P, -1, P).transpose(2, 1, 0, 3).reshape(-1, P, UNIT)

    def ffn_units(gate, up, down):
        g, u, d = columns(gate), columns(up), down.reshape(FT, P, UNIT)
        return [x for c in range(CHUNKS) for x in (g[2 * c], u[2 * c], g[2 * c + 1], u[2 * c + 1], d[2 * c], d[2 * c + 1])]

    w_in = columns(w["w_in"][0])
    v_units = w["w_in"][0][:, 1024:1536].reshape(4, 2, P, 512).transpose(0, 2, 1, 3).reshape(4, P, UNIT)
    units = ffn_units(w["ffn1_w_gate"][0], w["ffn1_w_up"][0], w["ffn1_w_down"][0])
    for p in range(PAIRS):
        units += [w_in[16 + p], w_in[12 + p], w_in[p], w_in[4 + p]]
    units += list(v_units)
    units += list(columns(w["w_out"][0])) * 2
    units += ffn_units(w["ffn2_w_gate"][0], w["ffn2_w_up"][0], w["ffn2_w_down"][0])
    units += [np.zeros((P, UNIT), np.float32)] * 4

    def tiles(v):
        return v.reshape(-1, P).T

    smalls = np.concatenate([
        tiles(w["ffn1_norm"][0]), tiles(w["mix_norm"][0]), tiles(w["ffn2_norm"][0]),
        w["conv_w"][0].reshape(TAPS, 4, P).transpose(2, 1, 0).reshape(P, 4 * TAPS),
        tiles(w["conv_b"][0]), tiles(w["conv_ln_g"][0]), tiles(w["conv_ln_b"][0]),
        np.tile(w["q_norm"][0], 2)[:, None], np.tile(w["k_norm"][0], 2)[:, None]], axis=1)

    head = np.arange(P) // DH
    cols = np.stack([np.full(P, 1.0 / D), (head == 0) / DH, (head == 1) / DH, np.full(P, 1.0 / 512)], 1).astype(np.float32)
    dist = np.arange(P)[:, None] + (SEQ - P) - np.arange(SEQ)[None, :]
    count = sum(((dist >= 0) & (dist <= window) & (dist % step == 0)).astype(int)
                for window, step in ((128, 1), (512, 4), (2048, 16)))
    table = np.where(count > 0, -np.log(np.maximum(count, 1)), -NEG).astype(np.float32)

    arrays = {
        "xT": w["x"][0].T.reshape(DT, P, SEQ).transpose(1, 0, 2),
        "stream": np.stack(units),
        "smalls": smalls,
        "cols": cols,
        "ident": np.eye(P, dtype=np.float32),
        "table": table,
    }
    arrays = {f"in_{k}": np.ascontiguousarray(v) for k, v in arrays.items()}
    nc = bacc.Bacc("TRN2", target_bir_lowering=False, num_devices=1)
    args = [nc.dram_tensor(k, a.shape, mybir.dt.from_np(a.dtype), kind="ExternalInput").ap() for k, a in arrays.items()]
    args.append(nc.dram_tensor("outT", (P, DT, SEQ), F32, kind="ExternalOutput").ap())
    build(nc, *args)
    r = run_bass_kernel_spmd(nc, [arrays], core_ids=[0])
    out = r.results[0]["outT"]
    return out.transpose(1, 0, 2).reshape(D, SEQ).T.reshape(1, SEQ, D)
```
